# Optimizing a Trainium2 kernel written in Bass

```python
import jax, jax.numpy as jnp
from jax import lax
import numpy as np

D_MODEL = 1024
BATCH = 1
SEQ = 512
DEPTH = 2

N_MIXERS = 2
SSD_EXPAND = 2
D_INNER = SSD_EXPAND * D_MODEL
HEAD_DIM = 64
N_SSD_HEADS = D_INNER // HEAD_DIM
N_SSD_GROUPS = 4
HEADS_PER_GROUP = N_SSD_HEADS // N_SSD_GROUPS
D_STATE = 128
SSD_CONV = 4
CHUNK = 128
D_XBC = D_INNER + 2 * N_SSD_GROUPS * D_STATE
D_IN_PROJ = D_INNER + D_XBC + N_SSD_HEADS
DT_MIN = 1e-3
DT_MAX = 1e-1
A_MIN = 1.0
A_MAX = 16.0
POOL_WINDOWS = (2, 4, 8, 16)
N_POOL_GROUPS = len(POOL_WINDOWS)
POOL_GROUP_DIM = D_MODEL // N_POOL_GROUPS
D_FF = 2816
FFN_CONV = 3
EPS = 1e-6

kernel_name = 'hybrid_ssd_pool_convffn_trunk'

def rms_norm(x, w):
    xf = x.astype(jnp.float32)
    xf = xf * lax.rsqrt(jnp.mean(xf * xf, axis=-1, keepdims=True) + EPS)
    return (xf * w.astype(jnp.float32)).astype(x.dtype)

def causal_depthwise_conv(x, w, b):
    k = w.shape[0]
    y = lax.conv_general_dilated(x, w[:, None, :].astype(x.dtype), window_strides=(1,),
                                 padding=[(k - 1, 0)],
                                 dimension_numbers=('NWC', 'WIO', 'NWC'),
                                 feature_group_count=x.shape[-1])
    return y + b.astype(x.dtype)

def segsum_decay(a_cum):
    q = a_cum.shape[-1]
    mask = jnp.tril(jnp.ones((q, q), dtype=bool))
    diff = a_cum[..., :, None] - a_cum[..., None, :]
    return jnp.exp(jnp.where(mask, diff, -jnp.inf))

def ssd_chunked(xh, dt, a, bm, cm):
    b, l, h, p = xh.shape
    g, n = bm.shape[2], bm.shape[3]
    r = h // g
    nc = l // CHUNK
    xf = xh.astype(jnp.float32).reshape(b, nc, CHUNK, g, r, p)
    dtc = dt.reshape(b, nc, CHUNK, g, r)
    bc = bm.astype(jnp.float32).reshape(b, nc, CHUNK, g, n)
    cc = cm.astype(jnp.float32).reshape(b, nc, CHUNK, g, n)
    a_dt = jnp.moveaxis(dtc * a.reshape(g, r), 2, -1)
    a_cum = jnp.cumsum(a_dt, axis=-1)
    xdt = xf * dtc[..., None]
    decay = segsum_decay(a_cum)
    cb = jnp.einsum('bclgn,bcsgn->bcgls', cc, bc)
    y_diag = jnp.einsum('bcgls,bcgrls,bcsgrp->bclgrp', cb, decay, xdt)
    decay_to_end = jnp.exp(a_cum[..., -1:] - a_cum)
    states = jnp.einsum('bcsgn,bcgrs,bcsgrp->bcgrpn', bc, decay_to_end, xdt)
    chunk_decay = jnp.exp(a_cum[..., -1])

    def step(carry, inp):
        st, dec = inp
        return carry * dec[..., None, None] + st, carry

    h0 = jnp.zeros((b, g, r, p, n), jnp.float32)
    _, prev = lax.scan(step, h0, (jnp.moveaxis(states, 1, 0), jnp.moveaxis(chunk_decay, 1, 0)))
    prev = jnp.moveaxis(prev, 0, 1)
    y_off = jnp.einsum('bclgn,bcgrpn,bcgrl->bclgrp', cc, prev, jnp.exp(a_cum))
    return (y_diag + y_off).reshape(b, l, h, p)

def ssd_mixer(u, w_in, conv_w, conv_b, dt_bias, a_log, d_skip, norm_w, w_out):
    b, l, _ = u.shape
    zxbcdt = u @ w_in.astype(u.dtype)
    z, xbc, dt = jnp.split(zxbcdt, [D_INNER, D_INNER + D_XBC], axis=-1)
    xbc = jax.nn.silu(causal_depthwise_conv(xbc, conv_w, conv_b))
    xs, bm, cm = jnp.split(xbc, [D_INNER, D_INNER + N_SSD_GROUPS * D_STATE], axis=-1)
    xh = xs.reshape(b, l, N_SSD_HEADS, HEAD_DIM)
    bm = bm.reshape(b, l, N_SSD_GROUPS, D_STATE)
    cm = cm.reshape(b, l, N_SSD_GROUPS, D_STATE)
    dt = jax.nn.softplus(dt.astype(jnp.float32) + dt_bias.astype(jnp.float32))
    a = -jnp.exp(a_log.astype(jnp.float32))
    y = ssd_chunked(xh, dt, a, bm, cm)
    y = y + d_skip.astype(jnp.float32)[:, None] * xh.astype(jnp.float32)
    y = y.reshape(b, l, D_INNER) * jax.nn.silu(z.astype(jnp.float32))
    yg = y.reshape(b, l, N_SSD_GROUPS, D_INNER // N_SSD_GROUPS)
    yg = yg * lax.rsqrt(jnp.mean(yg * yg, axis=-1, keepdims=True) + EPS)
    y = (yg.reshape(b, l, D_INNER) * norm_w.astype(jnp.float32)).astype(u.dtype)
    return y @ w_out.astype(u.dtype)

def pool_mixer(u, w_pool, scale):
    b, l, d = u.shape
    uf = u.astype(jnp.float32)
    cs = jnp.pad(jnp.cumsum(uf, axis=1), ((0, 0), (1, 0), (0, 0)))
    pos = jnp.arange(1, l + 1, dtype=jnp.float32)[None, :, None]
    groups = []
    for k, w in enumerate(POOL_WINDOWS):
        cg = cs[..., k * POOL_GROUP_DIM:(k + 1) * POOL_GROUP_DIM]
        lagged = jnp.pad(cg, ((0, 0), (w - 1, 0), (0, 0)))[:, :l]
        mean = (cg[:, 1:] - lagged) / jnp.minimum(pos, float(w))
        groups.append(mean - uf[..., k * POOL_GROUP_DIM:(k + 1) * POOL_GROUP_DIM])
    mixed = jnp.stack(groups, axis=2)
    out = jnp.einsum('blgc,gcd->blgd', mixed, w_pool.astype(jnp.float32)).reshape(b, l, d)
    return (out * scale.astype(jnp.float32)).astype(u.dtype)

def conv_ffn(u, w_up, conv_w, conv_b, w_down):
    h = u @ w_up.astype(u.dtype)
    h = causal_depthwise_conv(h, conv_w, conv_b)
    gate, val = jnp.split(h, 2, axis=-1)
    return (jax.nn.silu(gate) * val) @ w_down.astype(u.dtype)

def setup_inputs(seed: int = 0) -> dict:
    key = jax.random.key(seed)
    ks = jax.random.split(key, 24)
    n_ssd = (DEPTH + N_MIXERS - 1) // N_MIXERS
    n_pool = DEPTH // N_MIXERS
    nrm = jax.random.normal
    x = nrm(ks[0], (BATCH, SEQ, D_MODEL), jnp.float32)
    ssd_w_in = nrm(ks[1], (n_ssd, D_MODEL, D_IN_PROJ), jnp.float32) * D_MODEL ** -0.5
    ssd_conv_w = nrm(ks[2], (n_ssd, SSD_CONV, D_XBC), jnp.float32) * SSD_CONV ** -0.5
    ssd_conv_b = nrm(ks[3], (n_ssd, D_XBC), jnp.float32) * 0.01
    u = jax.random.uniform(ks[4], (n_ssd, N_SSD_HEADS), jnp.float32)
    dt0 = jnp.exp(u * (np.log(DT_MAX) - np.log(DT_MIN)) + np.log(DT_MIN))
    ssd_dt_bias = dt0 + jnp.log(-jnp.expm1(-dt0))
    ssd_a_log = jnp.log(jax.random.uniform(ks[5], (n_ssd, N_SSD_HEADS), jnp.float32, A_MIN, A_MAX))
    ssd_d = 1.0 + 0.1 * nrm(ks[6], (n_ssd, N_SSD_HEADS), jnp.float32)
    ssd_norm_w = 1.0 + 0.1 * nrm(ks[7], (n_ssd, D_INNER), jnp.float32)
    ssd_w_out = nrm(ks[8], (n_ssd, D_INNER, D_MODEL), jnp.float32) * D_INNER ** -0.5
    pool_w = nrm(ks[9], (n_pool, N_POOL_GROUPS, POOL_GROUP_DIM, POOL_GROUP_DIM), jnp.float32) * POOL_GROUP_DIM ** -0.5
    pool_scale = 1.0 + 0.1 * nrm(ks[10], (n_pool, D_MODEL), jnp.float32)
    ffn_w_up = nrm(ks[11], (DEPTH, D_MODEL, 2 * D_FF), jnp.float32) * D_MODEL ** -0.5
    ffn_conv_w = nrm(ks[12], (DEPTH, FFN_CONV, 2 * D_FF), jnp.float32) * FFN_CONV ** -0.5
    ffn_conv_b = nrm(ks[13], (DEPTH, 2 * D_FF), jnp.float32) * 0.01
    ffn_w_down = nrm(ks[14], (DEPTH, D_FF, D_MODEL), jnp.float32) * D_FF ** -0.5
    norm_mix_pre = 1.0 + 0.1 * nrm(ks[15], (DEPTH, D_MODEL), jnp.float32)
    norm_mix_post = 1.0 + 0.1 * nrm(ks[16], (DEPTH, D_MODEL), jnp.float32)
    norm_ffn_pre = 1.0 + 0.1 * nrm(ks[17], (DEPTH, D_MODEL), jnp.float32)
    norm_ffn_post = 1.0 + 0.1 * nrm(ks[18], (DEPTH, D_MODEL), jnp.float32)
    return {'x': x, 'ssd_w_in': ssd_w_in, 'ssd_conv_w': ssd_conv_w, 'ssd_conv_b': ssd_conv_b,
            'ssd_dt_bias': ssd_dt_bias, 'ssd_a_log': ssd_a_log, 'ssd_d': ssd_d,
            'ssd_norm_w': ssd_norm_w, 'ssd_w_out': ssd_w_out, 'pool_w': pool_w,
            'pool_scale': pool_scale, 'ffn_w_up': ffn_w_up, 'ffn_conv_w': ffn_conv_w,
            'ffn_conv_b': ffn_conv_b, 'ffn_w_down': ffn_w_down, 'norm_mix_pre': norm_mix_pre,
            'norm_mix_post': norm_mix_post, 'norm_ffn_pre': norm_ffn_pre,
            'norm_ffn_post': norm_ffn_post}

def reference(x, ssd_w_in, ssd_conv_w, ssd_conv_b, ssd_dt_bias, ssd_a_log, ssd_d,
              ssd_norm_w, ssd_w_out, pool_w, pool_scale, ffn_w_up, ffn_conv_w, ffn_conv_b,
              ffn_w_down, norm_mix_pre, norm_mix_post, norm_ffn_pre, norm_ffn_post):
    for i in range(DEPTH):
        j = i // N_MIXERS
        h = rms_norm(x, norm_mix_pre[i])
        if i % N_MIXERS == 0:
            mix = ssd_mixer(h, ssd_w_in[j], ssd_conv_w[j], ssd_conv_b[j], ssd_dt_bias[j],
                            ssd_a_log[j], ssd_d[j], ssd_norm_w[j], ssd_w_out[j])
        else:
            mix = pool_mixer(h, pool_w[j], pool_scale[j])
        x = x + rms_norm(mix, norm_mix_post[i])
        f = conv_ffn(rms_norm(x, norm_ffn_pre[i]), ffn_w_up[i], ffn_conv_w[i], ffn_conv_b[i],
                     ffn_w_down[i])
        x = x + rms_norm(f, norm_ffn_post[i])
    return x


_drawn_inputs = setup_inputs


def setup_inputs(seed=0):
    import zlib

    import numpy as np

    out = dict(_drawn_inputs(seed))
    spreads = {}
    factors = {'ssd_conv_b': 4.5, 'ffn_conv_b': 5.133}
    for name, (base, spread) in spreads.items():
        noise = np.random.default_rng([zlib.crc32(name.encode()), seed]).standard_normal(out[name].shape)
        drawn = base * np.exp(spread * noise) if base else spread * noise
        out[name] = __import__('jax').numpy.asarray(drawn.astype(out[name].dtype))
    for name, factor in factors.items():
        out[name] = (out[name] * factor).astype(out[name].dtype)
    return out
```

```python
from contextlib import ExitStack

import concourse.bass as bass
from concourse import mybir

F32 = mybir.dt.float32
F32R = mybir.dt.float32r
ALU = mybir.AluOpType
ACT = mybir.ActivationFunctionType

P = 128
EPS = 1e-6
POOL_WINDOWS = (2, 4, 8, 16)


def hybrid_trunk(nc, x, ssd_w_in, ssd_conv_w, ssd_conv_b, ssd_dt_bias, ssd_a_log, ssd_d, ssd_norm_w,
                 ssd_w_out, pool_w, pool_scale, ffn_w_up, ffn_conv_w, ffn_conv_b, ffn_w_down,
                 norm_mix_pre, norm_mix_post, norm_ffn_pre, norm_ffn_post, out):
    T, D = x.shape[1:]
    DB = D // P
    NCH = T // P
    D_INNER = ssd_w_out.shape[1]
    IB = D_INNER // P
    HEADS = ssd_a_log.shape[1]
    G = 4
    HPG = HEADS // G
    HD = D_INNER // HEADS
    D_XBC = ssd_conv_w.shape[2]
    CB = D_XBC // P
    SSD_TAPS = ssd_conv_w.shape[1]
    D_FF = ffn_w_down.shape[1]
    FB = D_FF // P
    FFN_TAPS = ffn_conv_w.shape[1]
    QPG = IB // G
    assert (T, DB, NCH, IB, HPG, HD, CB, FB) == (512, 8, 4, 16, 8, 64, 24, 22)

    SLAB = 2 * D
    BC_SLABS = (CB - IB) // 2
    X_SLABS = IB // 2
    Z_SLABS = IB // 2
    OUT_SLABS = IB // 2
    UP_SLABS = FB
    DOWN_SLABS = FB // 2
    S_DT = 0
    S_BC = 1
    S_X = S_BC + BC_SLABS
    S_Z = S_X + X_SLABS
    S_OUT = S_Z + Z_SLABS
    S_UP = [S_OUT + OUT_SLABS, 0]
    S_DOWN = [S_UP[0] + UP_SLABS, 0]
    S_POOL = S_DOWN[0] + DOWN_SLABS
    S_UP[1] = S_POOL + 1
    S_DOWN[1] = S_UP[1] + UP_SLABS

    w_in_slabs = ssd_w_in[0, :, 0:D_INNER + D_XBC].rearrange("(k p) (s n) -> s p k n", p=P, n=2 * P)
    w_out_slabs = ssd_w_out[0].rearrange("(s k p) n -> s p k n", k=2, p=P)
    w_up_slabs = [ffn_w_up[l].rearrange("(k p) (s n) -> s p k n", p=P, n=2 * P) for l in range(2)]
    w_down_slabs = [ffn_w_down[l].rearrange("(s k p) n -> s p k n", k=2, p=P) for l in range(2)]
    w_pool_slab = pool_w[0].rearrange("g (k p) n -> p g k n", p=P)
    w_dt = ssd_w_in[0, :, D_INNER + D_XBC:].rearrange("(k p) n -> p k n", p=P)

    ROWS = {}
    at = 0
    for name, n in (("conv_w", SSD_TAPS * CB), ("conv_b", CB), ("pool_scale", DB),
                    ("mix_pre", 2 * DB), ("mix_post", 2 * DB), ("ffn_pre", 2 * DB),
                    ("ffn_post", 2 * DB), ("ssd_norm", IB),
                    ("ffn_w", 2 * FFN_TAPS * 2 * FB), ("ffn_b", 2 * 2 * FB)):
        ROWS[name] = at
        at += n
    PAR_ROWS = at
    PAR_TILES = (PAR_ROWS + P - 1) // P
    par_sources = [
        ("conv_w", ssd_conv_w.rearrange("a t (b p) -> (a t b) p", p=P)),
        ("conv_b", ssd_conv_b.rearrange("a (b p) -> (a b) p", p=P)),
        ("pool_scale", pool_scale.rearrange("a (b p) -> (a b) p", p=P)),
        ("mix_pre", norm_mix_pre.rearrange("a (b p) -> (a b) p", p=P)),
        ("mix_post", norm_mix_post.rearrange("a (b p) -> (a b) p", p=P)),
        ("ffn_pre", norm_ffn_pre.rearrange("a (b p) -> (a b) p", p=P)),
        ("ffn_post", norm_ffn_post.rearrange("a (b p) -> (a b) p", p=P)),
        ("ssd_norm", ssd_norm_w.rearrange("a (b p) -> (a b) p", p=P)),
        ("ffn_w", ffn_conv_w.rearrange("a t (b p) -> (a t b) p", p=P)),
        ("ffn_b", ffn_conv_b.rearrange("a (b p) -> (a b) p", p=P)),
    ]
    par_pieces = []
    for name, src in par_sources:
        row, done, n = ROWS[name], 0, src.shape[0]
        while done < n:
            k = min(n - done, P - (row + done) % P)
            par_pieces.append(((row + done) // P, (row + done) % P, k, src[done:done + k, :]))
            done += k

    with ExitStack() as ctx:
        def sb(name, shape, dt=F32, scope=ctx):
            return scope.enter_context(nc.sbuf_tensor(name, shape, dt))

        def sem(name):
            return ctx.enter_context(nc.semaphore(name))

        bank = ctx.enter_context(nc.psum_tensor("bank", [P, 8, T], F32))

        xres = sb("xres", [P, DB, T])
        h_hi = sb("h_hi", [P, DB, T], F32R)
        h_lo = sb("h_lo", [P, DB, T], F32R)
        raw = [sb(f"raw{s}", [P, SLAB]) for s in range(2)]
        w_hi = [sb(f"w_hi{s}", [P, SLAB], F32R) for s in range(2)]
        w_lo = [sb(f"w_lo{s}", [P, SLAB], F32R) for s in range(2)]
        par = sb("par", [P, PAR_TILES * P])
        pool_post = sb("pool_post", [P, DB])
        ident = sb("ident", [P, P])
        upper = sb("upper", [P, P])
        ones = sb("ones", [P, P])
        eps = sb("eps", [P, 1])
        sq = sb("sq", [P, 2, T])
        sum_sq = sb("sum_sq", [P, T])
        rms = sb("rms", [P, NCH])
        rrms = sb("rrms", [P, NCH])
        rrms_all = sb("rrms_all", [P, T])
        tmp = sb("tmp", [P, 4, T])
        edge = sb("edge", [P, G, 16])

        with ExitStack() as scope:
            x_rows = sb("x_rows", [P, NCH, D], scope=scope)
            par_rows = sb("par_rows", [P, PAR_TILES, P], scope=scope)
        mixer = ExitStack()
        xbc = sb("xbc", [P, CB, T], scope=mixer)
        with ExitStack() as scope:
            b_tok = sb("b_tok", [P, T], scope=scope)
            b_feat = sb("b_feat", [P, T], scope=scope)
            cb_mask = sb("cb_mask", [P, T], scope=scope)
            x_feat = sb("x_feat", [P, T], scope=scope)
            xdt = sb("xdt", [P, 2, T], scope=scope)
            xdt_end = sb("xdt_end", [P, T], scope=scope)
            decay = sb("decay", [P, 2, T], scope=scope)
            from_start = sb("from_start", [P, T], scope=scope)
            gate = sb("gate", [P, 2, T], scope=scope)
            state = sb("state", [P, NCH - 1, P], scope=scope)
            sel = sb("sel", [HPG, HPG, P], F32R, scope=scope)
            ac_hi = sb("ac_hi", [HPG, T], F32R, scope=scope)
            ac_lo = sb("ac_lo", [HPG, T], F32R, scope=scope)
            SM = [P, NCH, HEADS]
            v_dt, e_dt, u_dt, d_dt, l_dt, z_dt = (sb(n, SM, scope=scope) for n in
                                                  ("v_dt", "e_dt", "u_dt", "d_dt", "l_dt", "z_dt"))
            dt, a_dt, a_cum, to_end, chunk_decay = (sb(n, SM, scope=scope) for n in
                                                    ("dt", "a_dt", "a_cum", "to_end", "chunk_decay"))
            a_dt_g = sb("a_dt_g", [P, NCH, HPG], scope=scope)
            heads_in = sb("heads_in", [P, 3, HEADS], scope=scope)
            neg_a = sb("neg_a", [P, HEADS], scope=scope)
            d_pair = sb("d_pair", [P, IB], scope=scope)
            group_ms = sb("group_ms", [P, G, NCH], scope=scope)
        with ExitStack() as scope:
            group_scale = sb("group_scale", [P, G, T], scope=scope)
            y_hi = [sb(f"y_hi{s}", [P, 2, T], F32R, scope=scope) for s in range(2)]
            y_lo = [sb(f"y_lo{s}", [P, 2, T], F32R, scope=scope) for s in range(2)]
        mixer.close()
        with ExitStack() as scope:
            act_hi = sb("act_hi", [P, FB, T], F32R, scope=scope)
            act_lo = sb("act_lo", [P, FB, T], F32R, scope=scope)
        with ExitStack() as scope:
            out_rows = sb("out_rows", [P, NCH, D], scope=scope)

        slab_in = [sem("slab_in0"), sem("slab_in1")]
        hi_ready = sem("hi_ready")
        lo_ready = sem("lo_ready")
        mm_done = sem("mm_done")
        params_in, x_in, heads_loaded = sem("params_in"), sem("x_in"), sem("heads_loaded")
        consts, consts_step = sem("consts"), sem("consts_step")
        par_T, par_ready, x_T, xres_ready = sem("par_T"), sem("par_ready"), sem("x_T"), sem("xres_ready")
        sq_ready = sem("sq_ready")
        sum_step = sem("sum_step")
        tot_ready = sem("tot_ready")
        rms_ready = sem("rms_ready")
        rrms_ready = sem("rrms_ready")
        rb_ready = sem("rb_ready")
        rb_copied = sem("rb_copied")
        f0_ready = sem("f0_ready")
        x_updated = sem("x_updated")
        post_step = sem("post_step")
        hn_ready = sem("hn_ready")
        h_hi_ready = sem("h_hi_ready")
        h_ready = sem("h_ready")
        dt_zero, sel_zero, sel_made, sel_ready = sem("dt_zero"), sem("sel_zero"), sem("sel_made"), sem("sel_ready")
        dt_feat_ready, dt_T = sem("dt_feat_ready"), sem("dt_T")
        dt_vec, dt_act = sem("dt_vec"), sem("dt_act")
        cum_ready = sem("cum_ready")
        conv_tap = sem("conv_tap")
        conv_part = sem("conv_part")
        conv_done = sem("conv_done")
        conv_silu = sem("conv_silu")
        a_dt_g_ready, b_feat_ready = sem("a_dt_g_ready"), sem("b_feat_ready")
        acg_mm, b_tok_mm, cb_mm = sem("acg_mm"), sem("b_tok_mm"), sem("cb_mm")
        ac_hi_ready, b_tok_ready = sem("ac_hi_ready"), sem("b_tok_ready")
        ac_ready, cb_ready = sem("ac_ready"), sem("cb_ready")
        x_feat_ready, x_tok_mm = sem("x_feat_ready"), sem("x_tok_mm")
        xdt_ready, xdt_end_ready = sem("xdt_ready"), sem("xdt_end_ready")
        r_mm = sem("r_mm")
        diff_ready = sem("diff_ready")
        relu_ready, exp_ready = sem("relu_ready"), sem("exp_ready")
        m_ready = sem("m_ready")
        fs_mm, fs_ready = sem("fs_mm"), sem("fs_ready")
        st_mm = sem("st_mm")
        st_step = sem("st_step")
        yo_mm, yd_mm = sem("yo_mm"), sem("yd_mm")
        gate_ready = sem("gate_ready")
        y_step = sem("y_step")
        y_done = sem("y_done")
        ysq_ready, gsum_step = sem("ysq_ready"), sem("gsum_step")
        y_seen = sem("y_seen")
        gtot_mm, gtot_ready = sem("gtot_mm"), sem("gtot_ready")
        grms_ready, grrms_ready, grb_mm = sem("grms_ready"), sem("grrms_ready"), sem("grb_mm")
        group_scale_ready = sem("group_scale_ready")
        yn_ready, y_hi_ready, y_ready = sem("yn_ready"), sem("y_hi_ready"), sem("y_ready")
        gate_silu = sem("gate_silu")
        u_ready = sem("u_ready")
        act_hi_ready, act_ready = sem("act_hi_ready"), sem("act_ready")
        win_step = sem("win_step")
        out_T, out_copied, out_stored = sem("out_T"), sem("out_copied"), sem("out_stored")

        PRIMED = {
            "tensor": [acg_mm, cb_mm, x_tok_mm, fs_mm, st_mm, yd_mm, yo_mm, gtot_mm],
            "scalar": [gtot_ready, gate_ready, fs_ready],
            "vector": [st_step, y_step, diff_ready, y_done, gsum_step, u_ready, act_ready],
        }

        def prime(eng, name):
            for s in PRIMED[name]:
                eng.sem_inc(s, 1)

        def col(name, i):
            c = ROWS[name] + i
            return par[:, c:c + 1] if isinstance(i, int) else par[:, bass.ds(c, 1)]

        def by_cols(tile):
            return tile[:].rearrange("p (k n) -> p k n", n=2 * P)

        def by_rows(tile):
            return tile[:].rearrange("p (k n) -> p k n", n=D)

        def chunked(ap, n=P):
            return ap.rearrange("p (c l) -> p c l", l=n)

        def load(sp, n0, i, source, view):
            if not (isinstance(i, int) and n0 + 2 * i < 2):
                sp.wait_ge(lo_ready, n0 - 1 + 2 * i)
            sp.dma_start(view(raw[n0 % 2]), source).then_inc(slab_in[n0 % 2], 16)

        def split_hi(act, n0, i):
            act.wait_ge(slab_in[n0 % 2], 16 * (n0 // 2 + 1) + 16 * i)
            if not (isinstance(i, int) and n0 + 2 * i < 2):
                act.wait_ge(mm_done, 2 * (n0 - 1) + 4 * i)
            act.activation(w_hi[n0 % 2][:], raw[n0 % 2][:], ACT.Copy).then_inc(hi_ready, 1)

        def split_lo(dve, n0, i):
            dve.wait_ge(hi_ready, n0 + 1 + 2 * i)
            dve.tensor_tensor(w_lo[n0 % 2][:], raw[n0 % 2][:], w_hi[n0 % 2][:].bitcast(F32),
                              ALU.subtract).then_inc(lo_ready, 1)

        def three_passes(pe, dst, wh, wl, xh, xl, first, last, **kw):
            pe.matmul(dst, wh, xh, start=first, stop=False, **kw)
            pe.matmul(dst, wh, xl, start=False, stop=False, **kw)
            return pe.matmul(dst, wl, xh, start=False, stop=last, **kw)

        def block_product(pe, dst, slot, j):
            wh, wl, c = by_cols(w_hi[slot]), by_cols(w_lo[slot]), slice(j * P, (j + 1) * P)
            for k in range(DB):
                mm = three_passes(pe, dst, wh[:, k, c], wl[:, k, c], h_hi[:, k, :], h_lo[:, k, :],
                                  k == 0, k == DB - 1)
            return mm

        def norm_squares(act, m, source, scale=None):
            for b in range(DB):
                src = source(act, b)
                if b >= 2 or m > 0:
                    act.wait_ge(sum_step, 7 * m + (max(1, b - 2) if b >= 2 else 0))
                act.activation(sq[:, b % 2, :], src, ACT.Square,
                               scale=1.0 if scale is None else scale(b)).then_inc(sq_ready, 1)

        def norm_rms(act, m):
            act.wait_ge(tot_ready, m + 1)
            act.activation(rms[:, :], bank[:, 0, 0:NCH], ACT.Sqrt, bias=eps[:, 0:1],
                           scale=1.0 / D).then_inc(rms_ready, 1)

        def norm_sum(dve, m):
            for b in range(1, DB):
                dve.wait_ge(sq_ready, 8 * m + b + 1)
                if b == 1:
                    dve.tensor_tensor(sum_sq[:, :], sq[:, 0, :], sq[:, 1, :], ALU.add).then_inc(sum_step, 1)
                else:
                    dve.wait_ge(sum_step, 7 * m + b - 1)
                    dve.tensor_tensor(sum_sq[:, :], sum_sq[:, :], sq[:, b % 2, :],
                                      ALU.add).then_inc(sum_step, 1)
            dve.wait_ge(rms_ready, m + 1)
            dve.reciprocal(rrms[:, :], rms[:, :]).then_inc(rrms_ready, 1)

        def norm_spread(pe, m):
            pe.wait_ge(sum_step, 7 * m + 7)
            for c in range(NCH):
                mm = pe.matmul(bank[:, 0, c:c + 1], sum_sq[:, c * P:(c + 1) * P], ones[:, 0:1],
                               start=True, stop=True)
            mm.then_inc(tot_ready, 1)
            pe.wait_ge(rrms_ready, m + 1)
            for c in range(NCH):
                mm = pe.matmul(bank[:, 0, c * P:(c + 1) * P], rrms[:, c:c + 1].to_broadcast([P, P]),
                               ident[:, :], start=True, stop=True)
            mm.then_inc(rb_ready, 1)

        def pre_norm_act(act, u):
            def source(act, b):
                if u == 0:
                    act.wait_ge(xres_ready, DB)
                else:
                    act.wait_ge(x_updated, DB * (u - 1) + b + 1)
                return xres[:, b, :]
            norm_squares(act, 2 * u, source)
            norm_rms(act, 2 * u)
            for b in range(DB):
                act.wait_ge(hn_ready, DB * u + b + 1)
                act.activation(h_hi[:, b, :], tmp[:, b % 2, :], ACT.Copy).then_inc(h_hi_ready, 1)

        def pre_norm_low(dve, u, b):
            dve.wait_ge(h_hi_ready, DB * u + b + 1)
            dve.tensor_tensor(h_lo[:, b, :], tmp[:, b % 2, :], h_hi[:, b, :].bitcast(F32),
                              ALU.subtract).then_inc(h_ready, 1)

        def pre_norm_dve(dve, u, weight, windows=None):
            norm_sum(dve, 2 * u)
            dve.wait_ge(rb_ready, 2 * u + 1)
            for b in range(DB):
                if b >= 2:
                    dve.wait_ge(h_ready, DB * u + b - 1)
                ins = dve.scalar_tensor_tensor(tmp[:, b % 2, :], xres[:, b, :], weight(b), bank[:, 0, :],
                                               ALU.mult, ALU.mult)
                if windows is None:
                    ins.then_inc(hn_ready, 1)
                else:
                    windows(dve, b, ins)
                if b >= 1:
                    pre_norm_low(dve, u, b - 1)
            pre_norm_low(dve, u, DB - 1)

        def post_norm_act(act, u, mms, scale=None):
            act.wait_ge(mm_done, mms)
            if u > 0:
                act.wait_ge(x_updated, DB * u)
            act.activation(rrms_all[:, :], bank[:, 0, :], ACT.Copy).then_inc(f0_ready, 1)
            norm_squares(act, 2 * u + 1, lambda act, b: bank[:, b, :], scale)
            norm_rms(act, 2 * u + 1)

        def post_norm_dve(dve, u, weight):
            dve.wait_ge(f0_ready, u + 1)
            norm_sum(dve, 2 * u + 1)
            dve.tensor_scalar(tmp[:, 0, :], rrms_all[:, :], weight(0), None, ALU.mult).then_inc(post_step, 1)
            dve.wait_ge(rb_ready, 2 * u + 2)
            dve.wait_ge(post_step, 9 * u + 1)
            dve.tensor_tensor(tmp[:, 0, :], tmp[:, 0, :], bank[:, 0, :], ALU.mult).then_inc(post_step, 1)
            dve.tensor_copy(rrms_all[:, :], bank[:, 0, :]).then_inc(rb_copied, 1)
            dve.wait_ge(post_step, 9 * u + 2)
            dve.tensor_tensor(xres[:, 0, :], xres[:, 0, :], tmp[:, 0, :], ALU.add).then_inc(x_updated, 1)
            dve.wait_ge(rb_copied, u + 1)
            for b in range(1, DB):
                if b >= 2:
                    dve.wait_ge(x_updated, DB * u + b - 1)
                dve.scalar_tensor_tensor(tmp[:, b % 2, :], bank[:, b, :], weight(b), rrms_all[:, :],
                                         ALU.mult, ALU.mult).then_inc(post_step, 1)
                dve.wait_ge(post_step, 9 * u + 2 + b)
                dve.tensor_tensor(xres[:, b, :], xres[:, b, :], tmp[:, b % 2, :], ALU.add).then_inc(x_updated, 1)

        def last_tap(act, block, slot, w, b):
            act.activation(tmp[:, slot, :], bank[:, 4 + slot, :], ACT.Identity, bias=b,
                           scale=w).then_inc(conv_tap, 1)

        def other_taps(dve, count, part, slot, weights):
            dve.wait_ge(conv_tap, count + 1)
            n = len(weights)
            for j, w in enumerate(weights):
                back = j + 1
                if j:
                    dve.wait_ge(conv_part, part + j)
                dve.scalar_tensor_tensor(tmp[:, slot, back:], bank[:, 4 + slot, 0:T - back], w,
                                         tmp[:, slot, back:], ALU.mult, ALU.add
                                         ).then_inc(conv_part if j < n - 1 else conv_done, 1)

        def xbc_pe(pe, n0, i, it):
            for s in range(2):
                pe.wait_ge(lo_ready, n0 + s + 1 + 2 * i)
                for j in range(2):
                    q = 2 * s + j
                    if not isinstance(it, int) or it > 0:
                        pe.wait_ge(conv_done, 4 * it + q - 3)
                    block_product(pe, bank[:, 4 + q, :], (n0 + s) % 2, j).then_inc(mm_done, 1)

        def xbc_act(act, n0, i, it, blk):
            def finish(q):
                act.wait_ge(conv_done, 4 * it + q + 1)
                act.activation(xbc[:, blk + q, :], tmp[:, q, :], ACT.Silu).then_inc(conv_silu, 1)
            for s in range(2):
                split_hi(act, n0 + s + 1, i)
                for j in range(2):
                    q = 2 * s + j
                    act.wait_ge(mm_done, 2 * (n0 + s) + j + 1 + 4 * i)
                    if not isinstance(it, int) or it > 0:
                        act.wait_ge(conv_silu, 4 * it + q - 3)
                    last_tap(act, None, q, col("conv_w", (SSD_TAPS - 1) * CB + blk + q), col("conv_b", blk + q))
                    if q:
                        finish(q - 1)
            finish(3)

        def xbc_dve(dve, n0, i, it, blk):
            for s in range(2):
                split_lo(dve, n0 + s + 1, i)
                for j in range(2):
                    q = 2 * s + j
                    other_taps(dve, 4 * it + q, 2 * (4 * it + q), q,
                               [col("conv_w", t * CB + blk + q) for t in reversed(range(SSD_TAPS - 1))])

        def small(ap):
            return ap.rearrange("p (c h) -> p c h", h=HEADS)

        DT_STEPS = 16

        def dt_chain_act(act):
            act.wait_ge(sel_made, 1)
            act.activation(sel[:], decay[0:HPG, :, :].rearrange("r a (b n) -> r (a b) n", n=P),
                           ACT.Copy).then_inc(sel_ready, 1)
            act.wait_ge(heads_loaded, 48)
            act.activation(neg_a[:, :], heads_in[:, 1, :], ACT.Exp).then_inc(dt_act, 1)
            act.wait_ge(mm_done, 2)
            act.activation(gate[0:HEADS, 0, :], bank[0:HEADS, 1, :], ACT.Copy).then_inc(dt_feat_ready, 1)
            act.wait_ge(dt_vec, 1)
            act.activation(e_dt[:], v_dt[:], ACT.Abs).then_inc(dt_act, 1)
            act.wait_ge(dt_act, 2)
            act.activation(e_dt[:], e_dt[:], ACT.Exp, scale=-1.0).then_inc(dt_act, 1)
            act.wait_ge(dt_vec, 2)
            act.activation(l_dt[:], u_dt[:], ACT.Ln).then_inc(dt_act, 1)
            act.wait_ge(cum_ready, 1)
            act.activation(a_cum[:], small(bank[:, 2, 0:NCH * HEADS]), ACT.Copy).then_inc(dt_act, 1)
            act.activation(chunk_decay[:], small(bank[:, 3, 0:NCH * HEADS]), ACT.Exp).then_inc(dt_act, 1)
            act.wait_ge(dt_vec, DT_STEPS)
            act.activation(to_end[:], to_end[:], ACT.Exp).then_inc(dt_act, 1)

        def dt_chain_dve(dve):
            n = [0]

            def step(ins):
                n[0] += 1
                ins.then_inc(dt_vec, 1)
                dve.wait_ge(dt_vec, n[0])

            def over_chunks(row):
                return row.unsqueeze(1).to_broadcast([P, NCH, HEADS])

            dve.wait_ge(heads_loaded, 48)
            dve.wait_ge(dt_T, 1)
            step(dve.tensor_tensor(v_dt[:], small(bank[:, 1, 0:NCH * HEADS]), over_chunks(heads_in[:, 0, :]),
                                   ALU.add))
            dve.wait_ge(dt_act, 3)
            step(dve.tensor_scalar(u_dt[:], e_dt[:], 1.0, None, ALU.add))
            step(dve.tensor_scalar(d_dt[:], u_dt[:], -1.0, None, ALU.add))
            step(dve.tensor_scalar(z_dt[:], d_dt[:], 0.0, None, ALU.is_equal))
            step(dve.tensor_tensor(d_dt[:], d_dt[:], z_dt[:], ALU.add))
            step(dve.reciprocal(d_dt[:], d_dt[:]))
            step(dve.tensor_tensor(d_dt[:], d_dt[:], e_dt[:], ALU.mult))
            dve.wait_ge(dt_act, 4)
            step(dve.tensor_tensor(l_dt[:], l_dt[:], z_dt[:], ALU.add))
            step(dve.tensor_tensor(d_dt[:], d_dt[:], l_dt[:], ALU.mult))
            step(dve.tensor_scalar(v_dt[:], v_dt[:], 0.0, None, ALU.max))
            step(dve.tensor_tensor(dt[:], v_dt[:], d_dt[:], ALU.add))
            step(dve.tensor_scalar(neg_a[:, :], neg_a[:, :], -1.0, None, ALU.mult))
            step(dve.tensor_tensor(a_dt[:], dt[:], over_chunks(neg_a[:, :]), ALU.mult))
            pairs = heads_in[:, 2, :].rearrange("p (j h) -> p j h", h=2)
            step(dve.tensor_copy(d_pair[0:HD, :], pairs[0:HD, :, 0]))
            step(dve.tensor_copy(d_pair[HD:P, :], pairs[HD:P, :, 1]))
            dve.wait_ge(dt_act, 6)
            step(dve.tensor_tensor(to_end[:], small(bank[:, 3, 0:NCH * HEADS]), a_cum[:], ALU.subtract))
            assert n[0] == DT_STEPS

        def dt_chain_pe(pe):
            pe.wait_ge(lo_ready, S_DT + 1)
            pe.wait_ge(h_ready, DB)
            wh, wl = by_cols(w_hi[0]), by_cols(w_lo[0])
            for k in range(DB):
                mm = three_passes(pe, bank[:, 1, :], wh[:, k, 0:P], wl[:, k, 0:P], h_hi[:, k, :], h_lo[:, k, :],
                                  k == 0, k == DB - 1)
                if k % 4 == 3:
                    mm.then_inc(mm_done, 1)
            pe.wait_ge(dt_feat_ready, 1)
            for c in range(NCH):
                mm = pe.transpose(bank[:, 1, c * HEADS:(c + 1) * HEADS], gate[0:HEADS, 0, c * P:(c + 1) * P],
                                  ident[0:HEADS, 0:HEADS])
            mm.then_inc(dt_T, 1)
            pe.wait_ge(dt_vec, 13)
            rhs = a_dt[:].rearrange("p c h -> p (c h)")
            pe.matmul(bank[:, 2, 0:NCH * HEADS], upper[:], rhs, start=True, stop=True)
            pe.matmul(bank[:, 3, 0:NCH * HEADS], ones[:], rhs, start=True, stop=True).then_inc(cum_ready, 1)

        def cs(c):
            return slice(c * P, (c + 1) * P)

        def scan_pe(pe, g):
            pe.wait_ge(a_dt_g_ready, g + 1)
            pe.wait_ge(gtot_ready, 1 + g)
            for c in range(NCH):
                mm = pe.matmul(bank[0:HPG, 5, cs(c)], a_dt_g[:, c, :], upper[:], start=True, stop=True)
            mm.then_inc(acg_mm, 1)
            pe.wait_ge(b_feat_ready, g + 1)
            pe.wait_ge(st_step, 1 + 20 * g)
            for c in range(NCH):
                mm = pe.transpose(bank[:, 4, cs(c)], b_feat[:, cs(c)], ident[:])
            mm.then_inc(b_tok_mm, 1)
            pe.wait_ge(y_step, 1 + 12 * g)
            for c in range(NCH):
                mm = pe.matmul(bank[:, 6, cs(c)], b_feat[:, cs(c)],
                               xbc[:, IB + G + g, cs(c)] if isinstance(g, int) else
                               xbc[:, bass.ds(IB + G + g, 1), cs(c)].rearrange("p a l -> p (a l)"),
                               start=True, stop=True)
            mm.then_inc(cb_mm, 1)
            pe.wait_ge(b_tok_ready, g + 1)
            spread(pe, g, 0)
            for q in range(QPG):
                p = QPG * g + q
                if q % 2 == 0:
                    n = S_Z + q // 2
                    pe.wait_ge(lo_ready, n + 1 + 2 * g)
                    for j in range(2):
                        pe.wait_ge(gate_ready, 1 + p)
                        block_product(pe, bank[:, j, :], n % 2, j).then_inc(mm_done, 1)
                pe.wait_ge(xdt_end_ready, p + 1)
                for c in range(NCH - 1):
                    mm = pe.matmul(bank[:, 4, cs(c)], b_tok[:, cs(c)], xdt_end[:, cs(c)], start=True, stop=True)
                mm.then_inc(st_mm, 1)
                if q == 0:
                    pe.wait_ge(cb_ready, g + 1)
                else:
                    pe.wait_ge(y_step, 1 + 3 * p)
                pe.wait_ge(st_step, 1 + 5 * p + 5)
                for c in range(1, NCH):
                    mm = pe.matmul(bank[:, 6, cs(c)], state[:, c - 1, :],
                                   xbc[:, bass.ds(IB + G + g, 1), cs(c)].rearrange("p a l -> p (a l)"),
                                   start=True, stop=True)
                mm.then_inc(yo_mm, 1)
                pe.wait_ge(y_step, 1 + 3 * p)
                for h in range(2):
                    pe.wait_ge(m_ready, 2 * p + h + 1)
                    for c in range(NCH):
                        mm = pe.matmul(bank[h * HD:(h + 1) * HD, 7, cs(c)],
                                       xdt[:, q % 2, c * P + h * HD:c * P + (h + 1) * HD],
                                       decay[:, h, cs(c)], start=True, stop=True)
                mm.then_inc(yd_mm, 1)
                if q < QPG - 1:
                    spread(pe, g, q + 1)
            pe.wait_ge(gsum_step, 1 + 3 * g + 3)
            for c in range(NCH):
                mm = pe.matmul(bank[:, 5, c:c + 1], sum_sq[:, cs(c)], ones[:, 0:1], start=True, stop=True)
            mm.then_inc(gtot_mm, 1)

        def spread(pe, g, q):
            p = QPG * g + q
            pe.wait_ge(x_feat_ready, p + 1)
            pe.wait_ge(st_step, 1 + 5 * p)
            for c in range(NCH):
                mm = pe.transpose(bank[:, 4, cs(c)], x_feat[:, cs(c)], ident[:])
            mm.then_inc(x_tok_mm, 1)
            pe.wait_ge(ac_ready, g + 1)
            for h in range(2):
                pe.wait_ge(diff_ready, 1 + 2 * p)
                pe.matmul(bank[:, 2 + h, :], sel[:, 2 * q + h, :], ac_hi[:, :], start=True, stop=False)
                pe.matmul(bank[:, 2 + h, :], sel[:, 2 * q + h, :], ac_lo[:, :], start=False,
                          stop=True).then_inc(r_mm, 1)
            pe.wait_ge(fs_ready, 1 + p)
            pair = sel[:].rearrange("r b n -> r (b n)")[:, 2 * q * P + HD:2 * q * P + HD + P]
            pe.matmul(bank[:, 5, :], pair, ac_hi[:, :], start=True, stop=False)
            pe.matmul(bank[:, 5, :], pair, ac_lo[:, :], start=False, stop=True).then_inc(fs_mm, 1)

        def scan_act(act, g):
            def feat(dst, block, ready):
                act.activation(dst, xbc[:, bass.ds(block, 1), :].rearrange("p a l -> p (a l)"),
                               ACT.Copy).then_inc(ready, 1)

            def x_copy(q):
                p = QPG * g + q
                act.wait_ge(x_tok_mm, 1 + p)
                feat(x_feat[:, :], p, x_feat_ready)

            act.wait_ge(acg_mm, 1 + g)
            act.activation(a_dt_g[:], a_dt[:, :, bass.ds(HPG * g, HPG)], ACT.Copy).then_inc(a_dt_g_ready, 1)
            act.wait_ge(cb_mm, 1 + g)
            feat(b_feat[:, :], IB + g, b_feat_ready)
            x_copy(0)
            act.wait_ge(acg_mm, 1 + g + 1)
            act.wait_ge(fs_mm, 1 + QPG * g)
            act.activation(ac_hi[:, :], bank[0:HPG, 5, :], ACT.Copy).then_inc(ac_hi_ready, 1)
            act.wait_ge(b_tok_mm, g + 1)
            act.wait_ge(st_mm, 1 + QPG * g)
            act.activation(b_tok[:, :], bank[:, 4, :], ACT.Copy).then_inc(b_tok_ready, 1)
            for q in range(QPG):
                p = QPG * g + q
                for h in range(2):
                    act.wait_ge(diff_ready, 1 + 2 * p + h + 1)
                    act.activation(decay[:, h, :], decay[:, h, :], ACT.Relu).then_inc(relu_ready, 1)
                    act.wait_ge(relu_ready, 2 * p + h + 1)
                    act.activation(decay[:, h, :], decay[:, h, :], ACT.Exp, scale=-1.0).then_inc(exp_ready, 1)
                act.wait_ge(fs_mm, 1 + p + 1)
                act.wait_ge(y_step, 1 + 3 * p)
                act.activation(from_start[:, :], bank[:, 5, :], ACT.Exp).then_inc(fs_ready, 1)
                if q % 2 == 0:
                    split_hi(act, S_Z + q // 2 + 1, g)
                if q < QPG - 1:
                    x_copy(q + 1)
                act.wait_ge(mm_done, 2 * (S_Z + q // 2) + q % 2 + 1 + 4 * g)
                act.wait_ge(y_done, 1 + p)
                act.activation(gate[:, q % 2, :], bank[:, q % 2, :], ACT.Silu).then_inc(gate_ready, 1)
                act.wait_ge(y_done, 1 + p + 1)
                act.wait_ge(gsum_step, 1 + 3 * g + max(0, q - 2))
                act.sem_inc(y_seen, 1)
                act.activation(sq[:, q % 2, :], xbc[:, bass.ds(p, 1), :].rearrange("p a l -> p (a l)"),
                               ACT.Square).then_inc(ysq_ready, 1)
            act.wait_ge(gtot_mm, 1 + g + 1)
            act.activation(group_ms[:, bass.ds(g, 1), :].rearrange("p a c -> p (a c)"), bank[:, 5, 0:NCH],
                           ACT.Copy).then_inc(gtot_ready, 1)

        def scan_dve(dve, g):
            def heads(table, q, chunks=NCH):
                return table[:, 0:chunks, bass.ds(HPG * g + 2 * q, 2)].unsqueeze(3).to_broadcast(
                    [P, chunks, 2, HD])

            def by_head(ap):
                return ap.rearrange("p (c h d) -> p c h d", h=2, d=HD)

            dve.wait_ge(ac_hi_ready, g + 1)
            dve.tensor_tensor(ac_lo[:, :], bank[0:HPG, 5, :], ac_hi[:, :].bitcast(F32),
                              ALU.subtract).then_inc(ac_ready, 1)
            dve.wait_ge(cb_mm, 1 + g + 1)
            dve.tensor_tensor(chunked(cb_mask[:, :]), chunked(bank[:, 6, :]),
                              upper[:].unsqueeze(1).to_broadcast([P, NCH, P]), ALU.mult).then_inc(cb_ready, 1)
            dve.wait_ge(cb_ready, g + 1)
            for q in range(QPG):
                p = QPG * g + q
                dve.wait_ge(x_tok_mm, 1 + p + 1)
                dve.wait_ge(yd_mm, 1 + p)
                dve.tensor_tensor(by_head(xdt[:, q % 2, :]), by_head(bank[:, 4, :]), heads(dt, q),
                                  ALU.mult).then_inc(xdt_ready, 1)
                dve.wait_ge(xdt_ready, p + 1)
                dve.wait_ge(st_mm, 1 + p)
                dve.tensor_tensor(by_head(xdt_end[:, :]), by_head(xdt[:, q % 2, :]), heads(to_end, q),
                                  ALU.mult).then_inc(xdt_end_ready, 1)
                for h in range(2):
                    dve.wait_ge(r_mm, 2 * p + h + 1)
                    dve.tensor_tensor(chunked(decay[:, h, :]),
                                      a_cum[:, :, bass.ds(HPG * g + 2 * q + h, 1)].to_broadcast([P, NCH, P]),
                                      chunked(bank[:, 2 + h, :]), ALU.subtract).then_inc(diff_ready, 1)
                dve.wait_ge(st_mm, 1 + p + 1)
                dve.wait_ge(yo_mm, 1 + p)
                dve.tensor_copy(state[:, 0, :], bank[:, 4, 0:P]).then_inc(st_step, 1)
                for c in range(1, NCH - 1):
                    dve.wait_ge(st_step, 1 + 5 * p + 2 * c - 1)
                    dve.tensor_tensor(state[:, c, :].rearrange("p (h d) -> p h d", d=HD),
                                      state[:, c - 1, :].rearrange("p (h d) -> p h d", d=HD),
                                      chunk_decay[:, c, bass.ds(HPG * g + 2 * q, 2)].unsqueeze(2).to_broadcast(
                                          [P, 2, HD]), ALU.mult).then_inc(st_step, 1)
                    dve.wait_ge(st_step, 1 + 5 * p + 2 * c)
                    dve.tensor_tensor(state[:, c, :], state[:, c, :], bank[:, 4, cs(c)],
                                      ALU.add).then_inc(st_step, 1)
                for h in range(2):
                    dve.wait_ge(exp_ready, 2 * p + h + 1)
                    dve.tensor_tensor(decay[:, h, :], decay[:, h, :], cb_mask[:, :], ALU.mult).then_inc(m_ready, 1)
                if q % 2 == 0:
                    split_lo(dve, S_Z + q // 2 + 1, g)
                x_p = xbc[:, bass.ds(p, 1), :].rearrange("p a l -> p (a l)")
                dve.wait_ge(fs_ready, 1 + p + 1)
                dve.wait_ge(yo_mm, 1 + p + 1)
                dve.tensor_tensor(tmp[:, 1, P:], bank[:, 6, P:], from_start[:, P:], ALU.mult).then_inc(y_step, 1)
                dve.wait_ge(yd_mm, 1 + p + 1)
                dve.scalar_tensor_tensor(tmp[:, 0, :], x_p, d_pair[:, bass.ds(p, 1)], bank[:, 7, :],
                                         ALU.mult, ALU.add).then_inc(y_step, 1)
                dve.wait_ge(y_step, 1 + 3 * p + 2)
                dve.tensor_tensor(tmp[:, 0, P:], tmp[:, 0, P:], tmp[:, 1, P:], ALU.add).then_inc(y_step, 1)
                dve.wait_ge(y_step, 1 + 3 * p + 3)
                dve.wait_ge(gate_ready, 1 + p + 1)
                dve.tensor_tensor(x_p, tmp[:, 0, :], gate[:, q % 2, :], ALU.mult).then_inc(y_done, 1)
                if q >= 1:
                    dve.wait_ge(ysq_ready, p + 1)
                    if q == 1:
                        dve.wait_ge(gtot_mm, 1 + g)
                        dve.tensor_tensor(sum_sq[:, :], sq[:, 0, :], sq[:, 1, :], ALU.add).then_inc(gsum_step, 1)
                    else:
                        dve.wait_ge(gsum_step, 1 + 3 * g + q - 1)
                        dve.tensor_tensor(sum_sq[:, :], sum_sq[:, :], sq[:, q % 2, :],
                                          ALU.add).then_inc(gsum_step, 1)

        def group_norm_act(act):
            act.wait_ge(gtot_ready, 1 + G)
            act.activation(group_ms[:], group_ms[:], ACT.Sqrt, bias=eps[:, 0:1],
                           scale=1.0 / (D_INNER // G)).then_inc(grms_ready, 1)
            act.wait_ge(grb_mm, 1)
            act.activation(group_scale[:], bank[:, 0:G, :], ACT.Copy).then_inc(group_scale_ready, 1)

        def group_norm_dve(dve):
            dve.wait_ge(grms_ready, 1)
            dve.reciprocal(group_ms[:], group_ms[:]).then_inc(grrms_ready, 1)

        def group_norm_pe(pe):
            pe.wait_ge(grrms_ready, 1)
            for g in range(G):
                for c in range(NCH):
                    mm = pe.matmul(bank[:, g, cs(c)], group_ms[:, g, c:c + 1].to_broadcast([P, P]), ident[:],
                                   start=True, stop=True)
            mm.then_inc(grb_mm, 1)

        def y_split_act(act, n0, i, blk):
            for k in range(2):
                act.wait_ge(yn_ready, blk + k + 1)
                if not (isinstance(i, int) and n0 + 2 * i < S_OUT + 2):
                    act.wait_ge(mm_done, 2 * (n0 - 1) + 4 * i)
                act.activation(y_hi[n0 % 2][:, k, :], tmp[:, 2 * (n0 % 2) + k, :], ACT.Copy).then_inc(y_hi_ready, 1)

        def y_split_dve(dve, n0, i, blk, g):
            for k in range(2):
                s = 2 * (n0 % 2) + k
                if isinstance(blk, int):
                    y_b, scale = xbc[:, blk + k, :], group_scale[:, g, :]
                else:
                    y_b = xbc[:, bass.ds(blk + k, 1), :].rearrange("p a l -> p (a l)")
                    scale = group_scale[:, bass.ds(g, 1), :].rearrange("p a l -> p (a l)")
                dve.scalar_tensor_tensor(tmp[:, s, :], y_b, col("ssd_norm", blk + k), scale, ALU.mult,
                                         ALU.mult).then_inc(yn_ready, 1)
            for k in range(2):
                s = 2 * (n0 % 2) + k
                dve.wait_ge(y_hi_ready, blk + k + 1)
                dve.tensor_tensor(y_lo[n0 % 2][:, k, :], tmp[:, s, :], y_hi[n0 % 2][:, k, :].bitcast(F32),
                                  ALU.subtract).then_inc(y_ready, 1)

        def rows_product(pe, slot, k, xh, xl, first, last):
            wh, wl = by_rows(w_hi[slot]), by_rows(w_lo[slot])
            for b in range(DB):
                mm = three_passes(pe, bank[:, b, :], wh[:, k, b * P:(b + 1) * P], wl[:, k, b * P:(b + 1) * P],
                                  xh, xl, first, last)
            return mm

        def out_pe(pe, n0, i, blk, first=False, last=False):
            pe.wait_ge(lo_ready, n0 + 1 + 2 * i)
            for k in range(2):
                pe.wait_ge(y_ready, blk + k + 1)
                rows_product(pe, n0 % 2, k, y_hi[n0 % 2][:, k, :], y_lo[n0 % 2][:, k, :],
                             first and k == 0, last and k == 1).then_inc(mm_done, 1)

        CONV0 = [CB, CB + 2 * FB]
        PART0 = [2 * CB, 2 * CB + 2 * FB]

        def up_pe(pe, l, i):
            for s in range(2):
                pe.wait_ge(lo_ready, S_UP[l] + s + 1 + 2 * i)
                for j in range(2):
                    q = 2 * s + j
                    pe.wait_ge(conv_done, CONV0[l] + q - 3 + 4 * i)
                    block_product(pe, bank[:, 4 + q, :], (S_UP[l] + s) % 2, j).then_inc(mm_done, 1)

        def up_act(act, l, i):
            for s in range(2):
                split_hi(act, S_UP[l] + s + 1, i)
                for j in range(2):
                    q, blk = 2 * s + j, s * FB + j
                    act.wait_ge(mm_done, 2 * (S_UP[l] + s) + j + 1 + 4 * i)
                    if s == 0:
                        act.wait_ge(u_ready, 1 + FB * l + 2 * i)
                    else:
                        act.wait_ge(act_ready, 1 + FB * l + 2 * i)
                    last_tap(act, None, q, col("ffn_w", (l * FFN_TAPS + FFN_TAPS - 1) * 2 * FB + blk + 2 * i),
                             col("ffn_b", l * 2 * FB + blk + 2 * i))
                if s == 0:
                    for j in range(2):
                        act.wait_ge(conv_done, CONV0[l] + j + 1 + 4 * i)
                        act.activation(tmp[:, j, :], tmp[:, j, :], ACT.Silu).then_inc(gate_silu, 1)
            for j in range(2):
                act.wait_ge(u_ready, 1 + FB * l + j + 1 + 2 * i)
                act.activation(act_hi[:, bass.ds(2 * i + j, 1), :].rearrange("p a l -> p (a l)"),
                               tmp[:, 2 + j, :], ACT.Copy).then_inc(act_hi_ready, 1)

        def up_dve(dve, l, i):
            for s in range(2):
                split_lo(dve, S_UP[l] + s + 1, i)
                for j in range(2):
                    q, blk = 2 * s + j, s * FB + j
                    other_taps(dve, CONV0[l] + q + 4 * i, PART0[l] + q + 4 * i, q,
                               [col("ffn_w", (l * FFN_TAPS + t) * 2 * FB + blk + 2 * i)
                                for t in reversed(range(FFN_TAPS - 1))])
            for j in range(2):
                dve.wait_ge(gate_silu, FB * l + j + 1 + 2 * i)
                dve.wait_ge(conv_done, CONV0[l] + 2 + j + 1 + 4 * i)
                dve.tensor_tensor(tmp[:, 2 + j, :], tmp[:, j, :], tmp[:, 2 + j, :], ALU.mult).then_inc(u_ready, 1)
            for j in range(2):
                blk = bass.ds(2 * i + j, 1)
                dve.wait_ge(act_hi_ready, FB * l + j + 1 + 2 * i)
                dve.tensor_tensor(act_lo[:, blk, :].rearrange("p a l -> p (a l)"), tmp[:, 2 + j, :],
                                  act_hi[:, blk, :].rearrange("p a l -> p (a l)").bitcast(F32),
                                  ALU.subtract).then_inc(act_ready, 1)

        def down_pe(pe, l, s0, i, first=False, last=False):
            n0 = S_DOWN[l] + s0
            pe.wait_ge(lo_ready, n0 + 1 + 2 * i)
            for k in range(2):
                if isinstance(i, int):
                    blk = 2 * s0 + 4 * i + k
                    xh, xl = act_hi[:, blk, :], act_lo[:, blk, :]
                else:
                    blk = bass.ds(2 * s0 + k + 4 * i, 1)
                    xh = act_hi[:, blk, :].rearrange("p a l -> p (a l)")
                    xl = act_lo[:, blk, :].rearrange("p a l -> p (a l)")
                rows_product(pe, n0 % 2, k, xh, xl, first and k == 0, last and k == 1).then_inc(mm_done, 1)

        WIN_STEPS = []

        def pool_windows(dve, b, normed):
            n, g = WIN_STEPS[b], b // 2
            w = POOL_WINDOWS[g]

            def step(ins):
                nonlocal n
                n += 1
                ins.then_inc(win_step, 1)
                dve.wait_ge(win_step, n)
            step(normed)
            src, back, slot = tmp[:, b % 2, :], 1, 2
            while back < w:
                step(dve.tensor_tensor(tmp[:, slot, back:], src[:, back:], src[:, 0:T - back], ALU.add))
                step(dve.tensor_copy(tmp[:, slot, 0:back], src[:, 0:back]))
                src, back, slot = tmp[:, slot, :], 2 * back, 5 - slot
            step(dve.tensor_tensor(src[:, 0:16], src[:, 0:16], edge[:, g, :], ALU.mult))
            assert n == WIN_STEPS[b + 1]
            dve.scalar_tensor_tensor(tmp[:, b % 2, :], src, 1.0 / w, tmp[:, b % 2, :], ALU.mult,
                                     ALU.subtract).then_inc(hn_ready, 1)

        steps = 0
        for b in range(DB + 1):
            WIN_STEPS.append(steps)
            if b < DB:
                steps += 2 + 2 * (POOL_WINDOWS[b // 2].bit_length() - 1)

        def pool_pe(pe):
            pe.wait_ge(lo_ready, S_POOL + 1)
            pe.wait_ge(h_ready, 3 * DB)
            wh, wl = (t[S_POOL % 2][:].rearrange("p (g k n) -> p g k n", g=G, k=2) for t in (w_hi, w_lo))
            for b in range(DB):
                g, c = b // 2, slice((b % 2) * P, (b % 2 + 1) * P)
                for k in range(2):
                    mm = three_passes(pe, bank[:, b, :], wh[:, g, k, c], wl[:, g, k, c], h_hi[:, 2 * g + k, :],
                                      h_lo[:, 2 * g + k, :], k == 0, k == 1)
                if b % 4 == 3:
                    mm.then_inc(mm_done, 1)

        def norm_col(name, l):
            return lambda b: col(name, l * DB + b)

        block = ctx.enter_context(nc.Block())

        @block.sync
        def _(sp):
            sp.dma_start(x_rows[:], x[0].rearrange("(c p) d -> p c d", p=P)).then_inc(x_in, 16)
            sp.wait_ge(consts, 1)
            for t, r, n, src in par_pieces:
                sp.dma_start(par_rows[r:r + n, t, :], src).then_inc(params_in, 16)
            sp.wait_ge(dt_zero, 1)
            sp.dma_start(by_cols(raw[0])[:, :, 0:HEADS], w_dt).then_inc(slab_in[0], 16)
            load(sp, 1, 0, w_in_slabs[Z_SLABS + X_SLABS], by_cols)
            sp.wait_ge(x_T, DB)
            sp.wait_ge(par_T, 1)
            for j, src in enumerate((ssd_dt_bias, ssd_a_log, ssd_d)):
                sp.dma_start(heads_in[:, j, :], src[0:1, :].to_broadcast([P, HEADS])).then_inc(heads_loaded, 16)
            for s in range(1, BC_SLABS):
                load(sp, S_BC + s, 0, w_in_slabs[Z_SLABS + X_SLABS + s], by_cols)
            with sp.Fori(0, X_SLABS // 2) as i:
                for s in range(2):
                    load(sp, S_X + s, i, w_in_slabs[Z_SLABS + s + 2 * i], by_cols)
            with sp.Fori(0, Z_SLABS // 2) as i:
                for s in range(2):
                    load(sp, S_Z + s, i, w_in_slabs[s + 2 * i], by_cols)
            with sp.Fori(0, OUT_SLABS // 2) as i:
                for s in range(2):
                    load(sp, S_OUT + s, i, w_out_slabs[s + 2 * i], by_rows)
            for l in range(2):
                with sp.Fori(0, UP_SLABS // 2) as i:
                    for s in range(2):
                        load(sp, S_UP[l] + s, i, w_up_slabs[l][s * UP_SLABS // 2 + i], by_cols)
                with sp.Fori(0, DOWN_SLABS // 2) as i:
                    for s in range(2):
                        load(sp, S_DOWN[l] + s, i, w_down_slabs[l][s + 2 * i], by_rows)
                load(sp, S_DOWN[l] + DOWN_SLABS - 1, 0, w_down_slabs[l][DOWN_SLABS - 1], by_rows)
                if l == 0:
                    load(sp, S_POOL, 0, w_pool_slab,
                         lambda tile: tile[:].rearrange("p (g k n) -> p g k n", g=G, k=2))
            rows = out[0].rearrange("(c p) d -> c p d", p=P)
            for c in range(NCH):
                sp.wait_ge(out_copied, c + 1)
                sp.dma_start(rows[c], out_rows[:, c, :]).then_inc(out_stored, 16)
            sp.wait_ge(out_stored, 16 * NCH)

        @block.gpsimd
        def _(pool):
            n = [0]

            def step(ins):
                n[0] += 1
                ins.then_inc(consts_step, 1)
                pool.wait_ge(consts_step, n[0])
            step(pool.memset(ident[:], 0.0))
            step(pool.memset(ones[:], 1.0))
            step(pool.memset(eps[:], EPS))
            step(pool.affine_select(out=ident[:], in_=ident[:], compare_op=ALU.not_equal, fill=1.0, base=0,
                                    pattern=[[-1, P]], channel_multiplier=1))
            step(pool.affine_select(out=upper[:], in_=ones[:], compare_op=ALU.is_ge, fill=0.0, base=0,
                                    pattern=[[1, P]], channel_multiplier=-1))
            pool.memset(par_rows[:, PAR_TILES - 1, :], 0.0).then_inc(consts, 1)
            pool.memset(raw[0][:], 0.0).then_inc(dt_zero, 1)
            step(pool.memset(edge[:], 1.0))
            for g, w in enumerate(POOL_WINDOWS):
                for t in range(w - 1):
                    step(pool.memset(edge[:, g, t:t + 1], w / (t + 1)))
            pool.wait_ge(x_T, DB)
            pool.wait_ge(par_T, 1)
            rows = decay[0:HPG, :, :].rearrange("r a (b n) -> r (a b) n", n=P)
            pool.memset(rows, 0.0).then_inc(sel_zero, 1)
            pool.wait_ge(sel_zero, 1)
            pool.affine_select(out=rows, in_=rows, compare_op=ALU.not_equal, fill=1.0, base=0,
                               pattern=[[-1, HPG], [0, P]], channel_multiplier=1).then_inc(sel_made, 1)

        @block.tensor
        def _(pe):
            prime(pe, "tensor")
            pe.wait_ge(consts, 1)
            pe.wait_ge(x_in, 16)
            for b in range(DB):
                for c in range(NCH):
                    mm = pe.transpose(bank[:, b, cs(c)], x_rows[:, c, b * P:(b + 1) * P], ident[:])
                mm.then_inc(x_T, 1)
            pe.wait_ge(params_in, 16 * len(par_pieces))
            pe.wait_ge(xres_ready, DB)
            for t in range(PAR_TILES):
                mm = pe.transpose(bank[:, t // 4, cs(t % 4)], par_rows[:, t, :], ident[:])
            mm.then_inc(par_T, 1)
            pe.wait_ge(par_ready, 1)
            norm_spread(pe, 0)
            dt_chain_pe(pe)
            for it in range(BC_SLABS // 2):
                xbc_pe(pe, S_BC + 2 * it, 0, it)
            with pe.Fori(0, X_SLABS // 2) as i:
                xbc_pe(pe, S_X, i, BC_SLABS // 2 + i)
            pe.wait_ge(conv_done, CB)
            with pe.Fori(0, G) as g:
                scan_pe(pe, g)
            group_norm_pe(pe)
            pe.wait_ge(group_scale_ready, 1)
            for s in range(2):
                out_pe(pe, S_OUT + s, 0, 2 * s, first=s == 0)
            with pe.Fori(1, OUT_SLABS // 2 - 1) as i:
                for s in range(2):
                    out_pe(pe, S_OUT + s, i, 2 * s + 4 * i)
            for s in range(2):
                out_pe(pe, S_OUT + OUT_SLABS - 2 + s, 0, IB - 4 + 2 * s, last=s == 1)
            norm_spread(pe, 1)
            for l in range(2):
                if l == 1:
                    pe.wait_ge(x_updated, 2 * DB)
                    norm_spread(pe, 4)
                    pool_pe(pe)
                    norm_spread(pe, 5)
                pe.wait_ge(x_updated, DB * (2 * l + 1))
                norm_spread(pe, 4 * l + 2)
                pe.wait_ge(h_ready, DB * (2 * l + 2))
                with pe.Fori(0, UP_SLABS // 2) as i:
                    up_pe(pe, l, i)
                pe.wait_ge(act_ready, 1 + FB * (l + 1))
                for s in range(2):
                    down_pe(pe, l, s, 0, first=s == 0)
                with pe.Fori(1, DOWN_SLABS // 2) as i:
                    for s in range(2):
                        down_pe(pe, l, s, i)
                down_pe(pe, l, DOWN_SLABS - 1, 0, last=True)
                norm_spread(pe, 4 * l + 3)
            pe.wait_ge(x_updated, 4 * DB)
            for c in range(NCH):
                for b in range(DB):
                    mm = pe.transpose(bank[:, 2 * c + b // 4, cs(b % 4)], xres[:, b, cs(c)], ident[:])
                mm.then_inc(out_T, 1)

        @block.scalar
        def _(act):
            prime(act, "scalar")
            for b in range(0, DB, 2):
                act.wait_ge(x_T, b + 1)
                act.activation(xres[:, b, :], bank[:, b, :], ACT.Copy).then_inc(xres_ready, 1)
            split_hi(act, S_DT, 0)
            pre_norm_act(act, 0)
            dt_chain_act(act)
            split_hi(act, S_BC, 0)
            for it in range(BC_SLABS // 2):
                xbc_act(act, S_BC + 2 * it, 0, it, IB + 4 * it)
            with act.Fori(0, X_SLABS // 2) as i:
                xbc_act(act, S_X, i, BC_SLABS // 2 + i, 4 * i)
            with act.Fori(0, G) as g:
                scan_act(act, g)
            group_norm_act(act)
            for s in range(2):
                y_split_act(act, S_OUT + s, 0, 2 * s)
                split_hi(act, S_OUT + s + 1, 0)
            with act.Fori(1, OUT_SLABS // 2) as i:
                for s in range(2):
                    y_split_act(act, S_OUT + s, i, 2 * s + 4 * i)
                    split_hi(act, S_OUT + s + 1, i)
            post_norm_act(act, 0, 2 * S_UP[0])
            for l in range(2):
                if l == 1:
                    pre_norm_act(act, 2)
                    split_hi(act, S_UP[1], 0)
                    post_norm_act(act, 2, 2 * S_UP[1], lambda b: col("pool_scale", b))
                pre_norm_act(act, 2 * l + 1)
                with act.Fori(0, UP_SLABS // 2) as i:
                    up_act(act, l, i)
                with act.Fori(0, DOWN_SLABS // 2) as i:
                    for s in range(2):
                        split_hi(act, S_DOWN[l] + s + 1, i)
                if l == 0:
                    split_hi(act, S_POOL, 0)
                post_norm_act(act, 2 * l + 1, 2 * (S_DOWN[l] + DOWN_SLABS))
            for c in range(0, NCH, 1):
                act.wait_ge(out_T, c + 1)
                act.activation(out_rows[:, c, :].rearrange("p (b n) -> p b n", n=T), bank[:, 2 * c:2 * c + 2, :],
                               ACT.Copy).then_inc(out_copied, 1)

        @block.vector
        def _(dve):
            prime(dve, "vector")
            for b in range(1, DB, 2):
                dve.wait_ge(x_T, b + 1)
                dve.tensor_copy(xres[:, b, :], bank[:, b, :]).then_inc(xres_ready, 1)
            dve.wait_ge(par_T, 1)
            flat = bank[:, 0:2, :].rearrange("p b n -> p (b n)")
            dve.tensor_copy(par[:, :], flat[:, 0:PAR_TILES * P]).then_inc(par_ready, 1)
            dve.wait_ge(par_ready, 1)
            dve.tensor_tensor(pool_post[:, :], par[:, ROWS["pool_scale"]:ROWS["pool_scale"] + DB],
                              par[:, ROWS["mix_post"] + DB:ROWS["mix_post"] + 2 * DB], ALU.mult).then_inc(par_ready, 1)
            split_lo(dve, S_DT, 0)
            pre_norm_dve(dve, 0, norm_col("mix_pre", 0))
            dt_chain_dve(dve)
            split_lo(dve, S_BC, 0)
            for it in range(BC_SLABS // 2):
                xbc_dve(dve, S_BC + 2 * it, 0, it, IB + 4 * it)
            with dve.Fori(0, X_SLABS // 2) as i:
                xbc_dve(dve, S_X, i, BC_SLABS // 2 + i, 4 * i)
            dve.wait_ge(dt_act, 7)
            with dve.Fori(0, G) as g:
                scan_dve(dve, g)
            group_norm_dve(dve)
            dve.wait_ge(group_scale_ready, 1)
            for s in range(2):
                y_split_dve(dve, S_OUT + s, 0, 2 * s, 0)
                split_lo(dve, S_OUT + s + 1, 0)
            with dve.Fori(1, OUT_SLABS // 2) as i:
                for s in range(2):
                    y_split_dve(dve, S_OUT + s, i, 2 * s + 4 * i, i)
                    split_lo(dve, S_OUT + s + 1, i)
            post_norm_dve(dve, 0, norm_col("mix_post", 0))
            for l in range(2):
                if l == 1:
                    pre_norm_dve(dve, 2, norm_col("mix_pre", 1), pool_windows)
                    split_lo(dve, S_UP[1], 0)
                    dve.wait_ge(par_ready, 2)
                    post_norm_dve(dve, 2, lambda b: pool_post[:, b:b + 1])
                pre_norm_dve(dve, 2 * l + 1, norm_col("ffn_pre", l))
                with dve.Fori(0, UP_SLABS // 2) as i:
                    up_dve(dve, l, i)
                with dve.Fori(0, DOWN_SLABS // 2) as i:
                    for s in range(2):
                        split_lo(dve, S_DOWN[l] + s + 1, i)
                if l == 0:
                    split_lo(dve, S_POOL, 0)
                post_norm_dve(dve, 2 * l + 1, norm_col("ffn_post", l))


_OUTPUT = (1, 512, 1024)
_INPUTS = ["x", "ssd_w_in", "ssd_conv_w", "ssd_conv_b", "ssd_dt_bias", "ssd_a_log", "ssd_d", "ssd_norm_w",
           "ssd_w_out", "pool_w", "pool_scale", "ffn_w_up", "ffn_conv_w", "ffn_conv_b", "ffn_w_down",
           "norm_mix_pre", "norm_mix_post", "norm_ffn_pre", "norm_ffn_post"]


def kernel(**inputs):
    import numpy as np
    import concourse.bacc as bacc
    from concourse.bass_utils import run_bass_kernel_spmd

    nc = bacc.Bacc("TRN2", target_bir_lowering=False, num_devices=1)
    arrays, args = {}, []
    for name in _INPUTS:
        a = np.ascontiguousarray(inputs[name])
        arrays[f"in_{name}"] = a
        args.append(nc.dram_tensor(f"in_{name}", a.shape, mybir.dt.from_np(a.dtype), kind="ExternalInput").ap())
    args.append(nc.dram_tensor("result", _OUTPUT, F32, kind="ExternalOutput").ap())
    hybrid_trunk(nc, *args)
    return run_bass_kernel_spmd(nc, [arrays], core_ids=[0]).results[0]["result"]
```

```python
from contextlib import ExitStack

import concourse.bass as bass
from concourse import mybir

F32 = mybir.dt.float32
F32R = mybir.dt.float32r
ALU = mybir.AluOpType
ACT = mybir.ActivationFunctionType

P = 128
EPS = 1e-6
POOL_WINDOWS = (2, 4, 8, 16)


def hybrid_trunk(nc, x, ssd_w_in, ssd_conv_w, ssd_conv_b, ssd_dt_bias, ssd_a_log, ssd_d, ssd_norm_w,
                 ssd_w_out, pool_w, pool_scale, ffn_w_up, ffn_conv_w, ffn_conv_b, ffn_w_down,
                 norm_mix_pre, norm_mix_post, norm_ffn_pre, norm_ffn_post, out):
    T, D = x.shape[1:]
    DB = D // P
    NCH = T // P
    D_INNER = ssd_w_out.shape[1]
    IB = D_INNER // P
    HEADS = ssd_a_log.shape[1]
    G = 4
    HPG = HEADS // G
    HD = D_INNER // HEADS
    D_XBC = ssd_conv_w.shape[2]
    CB = D_XBC // P
    SSD_TAPS = ssd_conv_w.shape[1]
    D_FF = ffn_w_down.shape[1]
    FB = D_FF // P
    FFN_TAPS = ffn_conv_w.shape[1]
    QPG = IB // G
    assert (T, DB, NCH, IB, HPG, HD, CB, FB) == (512, 8, 4, 16, 8, 64, 24, 22)

    SLAB = 2 * D
    BC_SLABS = (CB - IB) // 2
    X_SLABS = IB // 2
    Z_SLABS = IB // 2
    OUT_SLABS = IB // 2
    UP_SLABS = FB
    DOWN_SLABS = FB // 2
    S_DT = 0
    S_BC = 1
    S_X = S_BC + BC_SLABS
    S_Z = S_X + X_SLABS
    S_OUT = S_Z + Z_SLABS
    S_UP = [S_OUT + OUT_SLABS, 0]
    S_DOWN = [S_UP[0] + UP_SLABS, 0]
    S_POOL = S_DOWN[0] + DOWN_SLABS
    S_UP[1] = S_POOL + 1
    S_DOWN[1] = S_UP[1] + UP_SLABS

    w_in_slabs = ssd_w_in[0, :, 0:D_INNER + D_XBC].rearrange("(k p) (s n) -> s p k n", p=P, n=2 * P)
    w_out_slabs = ssd_w_out[0].rearrange("(s k p) n -> s p k n", k=2, p=P)
    w_up_slabs = [ffn_w_up[l].rearrange("(k p) (s n) -> s p k n", p=P, n=2 * P) for l in range(2)]
    w_down_slabs = [ffn_w_down[l].rearrange("(s k p) n -> s p k n", k=2, p=P) for l in range(2)]
    w_pool_slab = pool_w[0].rearrange("g (k p) n -> p g k n", p=P)
    w_dt = ssd_w_in[0, :, D_INNER + D_XBC:].rearrange("(k p) n -> p k n", p=P)

    ROWS = {}
    at = 0
    for name, n in (("conv_w", SSD_TAPS * CB), ("conv_b", CB), ("pool_scale", DB),
                    ("mix_pre", 2 * DB), ("mix_post", 2 * DB), ("ffn_pre", 2 * DB),
                    ("ffn_post", 2 * DB), ("ssd_norm", IB),
                    ("ffn_w", 2 * FFN_TAPS * 2 * FB), ("ffn_b", 2 * 2 * FB)):
        ROWS[name] = at
        at += n
    PAR_ROWS = at
    PAR_TILES = (PAR_ROWS + P - 1) // P
    par_sources = [
        ("conv_w", ssd_conv_w.rearrange("a t (b p) -> (a t b) p", p=P)),
        ("conv_b", ssd_conv_b.rearrange("a (b p) -> (a b) p", p=P)),
        ("pool_scale", pool_scale.rearrange("a (b p) -> (a b) p", p=P)),
        ("mix_pre", norm_mix_pre.rearrange("a (b p) -> (a b) p", p=P)),
        ("mix_post", norm_mix_post.rearrange("a (b p) -> (a b) p", p=P)),
        ("ffn_pre", norm_ffn_pre.rearrange("a (b p) -> (a b) p", p=P)),
        ("ffn_post", norm_ffn_post.rearrange("a (b p) -> (a b) p", p=P)),
        ("ssd_norm", ssd_norm_w.rearrange("a (b p) -> (a b) p", p=P)),
        ("ffn_w", ffn_conv_w.rearrange("a t (b p) -> (a t b) p", p=P)),
        ("ffn_b", ffn_conv_b.rearrange("a (b p) -> (a b) p", p=P)),
    ]
    par_pieces = []
    for name, src in par_sources:
        row, done, n = ROWS[name], 0, src.shape[0]
        while done < n:
            k = min(n - done, P - (row + done) % P)
            par_pieces.append(((row + done) // P, (row + done) % P, k, src[done:done + k, :]))
            done += k

    with ExitStack() as ctx:
        def sb(name, shape, dt=F32, scope=ctx):
            return scope.enter_context(nc.sbuf_tensor(name, shape, dt))

        def sem(name):
            return ctx.enter_context(nc.semaphore(name))

        bank = ctx.enter_context(nc.psum_tensor("bank", [P, 8, T], F32))

        xres = sb("xres", [P, DB, T])
        h_hi = sb("h_hi", [P, DB, T], F32R)
        h_lo = sb("h_lo", [P, DB, T], F32R)
        raw = [sb(f"raw{s}", [P, SLAB]) for s in range(2)]
        w_hi = [sb(f"w_hi{s}", [P, SLAB], F32R) for s in range(2)]
        w_lo = [sb(f"w_lo{s}", [P, SLAB], F32R) for s in range(2)]
        par = sb("par", [P, PAR_TILES * P])
        pool_post = sb("pool_post", [P, DB])
        ident = sb("ident", [P, P])
        upper = sb("upper", [P, P])
        ones = sb("ones", [P, P])
        eps = sb("eps", [P, 1])
        sq = sb("sq", [P, 2, T])
        sum_sq = sb("sum_sq", [P, T])
        rms = sb("rms", [P, NCH])
        rrms = sb("rrms", [P, NCH])
        rrms_all = sb("rrms_all", [P, T])
        tmp = sb("tmp", [P, 4, T])
        edge = sb("edge", [P, G, 16])

        with ExitStack() as scope:
            x_rows = sb("x_rows", [P, NCH, D], scope=scope)
            par_rows = sb("par_rows", [P, PAR_TILES, P], scope=scope)
        mixer = ExitStack()
        xbc = sb("xbc", [P, CB, T], scope=mixer)
        with ExitStack() as scope:
            b_tok = sb("b_tok", [P, T], scope=scope)
            b_feat = sb("b_feat", [P, T], scope=scope)
            cb_mask = sb("cb_mask", [P, T], scope=scope)
            x_feat = sb("x_feat", [P, T], scope=scope)
            xdt = sb("xdt", [P, 2, T], scope=scope)
            xdt_end = sb("xdt_end", [P, T], scope=scope)
            decay = sb("decay", [P, 2, T], scope=scope)
            from_start = sb("from_start", [P, 2, T], scope=scope)
            gate = sb("gate", [P, 2, T], scope=scope)
            state = sb("state", [P, NCH - 1, P], scope=scope)
            sel = sb("sel", [HPG, HPG, P], F32R, scope=scope)
            ac_hi = sb("ac_hi", [HPG, T], F32R, scope=scope)
            ac_lo = sb("ac_lo", [HPG, T], F32R, scope=scope)
            SM = [P, NCH, HEADS]
            v_dt, e_dt, u_dt, d_dt, l_dt, z_dt = (sb(n, SM, scope=scope) for n in
                                                  ("v_dt", "e_dt", "u_dt", "d_dt", "l_dt", "z_dt"))
            dt, a_dt, a_cum, to_end, chunk_decay = (sb(n, SM, scope=scope) for n in
                                                    ("dt", "a_dt", "a_cum", "to_end", "chunk_decay"))
            a_dt_g = sb("a_dt_g", [P, NCH, HPG], scope=scope)
            heads_in = sb("heads_in", [P, 3, HEADS], scope=scope)
            neg_a = sb("neg_a", [P, HEADS], scope=scope)
            d_pair = sb("d_pair", [P, IB], scope=scope)
            group_ms = sb("group_ms", [P, G + 1, NCH], scope=scope)
        with ExitStack() as scope:
            group_scale = sb("group_scale", [P, G, T], scope=scope)
            y_hi = [sb(f"y_hi{s}", [P, 2, T], F32R, scope=scope) for s in range(2)]
            y_lo = [sb(f"y_lo{s}", [P, 2, T], F32R, scope=scope) for s in range(2)]
        mixer.close()
        with ExitStack() as scope:
            act_hi = sb("act_hi", [P, FB, T], F32R, scope=scope)
            act_lo = sb("act_lo", [P, FB, T], F32R, scope=scope)
        with ExitStack() as scope:
            win = sb("win", [P, 3, max(POOL_WINDOWS) + T], scope=scope)
        with ExitStack() as scope:
            out_rows = sb("out_rows", [P, NCH, D], scope=scope)

        slab_in = [sem("slab_in0"), sem("slab_in1")]
        hi_ready = sem("hi_ready")
        lo_ready = sem("lo_ready")
        mm_done = sem("mm_done")
        params_in, x_in, heads_loaded = sem("params_in"), sem("x_in"), sem("heads_loaded")
        consts, consts_step = sem("consts"), sem("consts_step")
        par_T, par_ready, x_T, xres_ready = sem("par_T"), sem("par_ready"), sem("x_T"), sem("xres_ready")
        sq_ready = sem("sq_ready")
        sum_step = sem("sum_step")
        tot_ready = sem("tot_ready")
        rms_ready = sem("rms_ready")
        rrms_ready = sem("rrms_ready")
        rb_ready = sem("rb_ready")
        rb_copied = sem("rb_copied")
        f0_ready = sem("f0_ready")
        x_updated = sem("x_updated")
        post_step = sem("post_step")
        hn_ready = sem("hn_ready")
        h_hi_ready = sem("h_hi_ready")
        h_ready = sem("h_ready")
        dt_zero, sel_zero, sel_made, sel_ready = sem("dt_zero"), sem("sel_zero"), sem("sel_made"), sem("sel_ready")
        dt_feat_ready, dt_T = sem("dt_feat_ready"), sem("dt_T")
        dt_vec, dt_act = sem("dt_vec"), sem("dt_act")
        cum_ready = sem("cum_ready")
        conv_tap = sem("conv_tap")
        conv_part = sem("conv_part")
        conv_done = sem("conv_done")
        conv_silu = sem("conv_silu")
        a_dt_g_ready, b_feat_ready = sem("a_dt_g_ready"), sem("b_feat_ready")
        acg_mm, b_tok_mm, cb_mm = sem("acg_mm"), sem("b_tok_mm"), sem("cb_mm")
        ac_hi_ready, b_tok_ready = sem("ac_hi_ready"), sem("b_tok_ready")
        ac_ready, cb_ready = sem("ac_ready"), sem("cb_ready")
        x_feat_ready, x_tok_mm = sem("x_feat_ready"), sem("x_tok_mm")
        xdt_ready, xdt_end_ready = sem("xdt_ready"), sem("xdt_end_ready")
        r_mm = sem("r_mm")
        diff_ready = sem("diff_ready")
        relu_ready, exp_ready = sem("relu_ready"), sem("exp_ready")
        m_ready = sem("m_ready")
        fs_mm, fs_ready = sem("fs_mm"), sem("fs_ready")
        st_mm = sem("st_mm")
        st_step = sem("st_step")
        yo_mm, yd_mm = sem("yo_mm"), sem("yd_mm")
        gate_ready = sem("gate_ready")
        y_step = sem("y_step")
        y_done = sem("y_done")
        ysq_ready, gsum_step = sem("ysq_ready"), sem("gsum_step")
        y_seen = sem("y_seen")
        gtot_mm, gtot_ready = sem("gtot_mm"), sem("gtot_ready")
        grms_ready, grrms_ready, grb_mm = sem("grms_ready"), sem("grrms_ready"), sem("grb_mm")
        group_scale_ready = sem("group_scale_ready")
        yn_ready, y_hi_ready, y_ready = sem("yn_ready"), sem("y_hi_ready"), sem("y_ready")
        gate_silu = sem("gate_silu")
        u_ready = sem("u_ready")
        act_hi_ready, act_ready = sem("act_hi_ready"), sem("act_ready")
        scaled = sem("scaled")
        win_step = sem("win_step")
        pads_zero = sem("pads_zero")
        mixed = sem("mixed")
        out_T, out_copied, out_stored = sem("out_T"), sem("out_copied"), sem("out_stored")

        PRIMED = {
            "tensor": [acg_mm, cb_mm, x_tok_mm, fs_mm, st_mm, yd_mm, yo_mm, gtot_mm],
            "scalar": [gate_ready, fs_ready],
            "vector": [xdt_ready, st_step, y_step, diff_ready, y_done, gsum_step, u_ready, act_ready],
        }

        def prime(eng, name):
            for s in PRIMED[name]:
                eng.sem_inc(s, 1)

        def col(name, i):
            c = ROWS[name] + i
            return par[:, c:c + 1] if isinstance(i, int) else par[:, bass.ds(c, 1)]

        def by_cols(tile):
            return tile[:].rearrange("p (k n) -> p k n", n=2 * P)

        def by_rows(tile):
            return tile[:].rearrange("p (k n) -> p k n", n=D)

        def chunked(ap, n=P):
            return ap.rearrange("p (c l) -> p c l", l=n)

        MORE_UP = [6, 18]
        MORE_POOL = 12
        ORDER = [0, 4, 5, 6, 7, 1, 2, 3]

        def load(sp, n0, i, source, view):
            if not (isinstance(i, int) and n0 + 2 * i < 2):
                sp.wait_ge(lo_ready, n0 - 1 + 2 * i)
            sp.dma_start(view(raw[n0 % 2]), source).then_inc(slab_in[n0 % 2], 16)

        def split_hi(act, n0, i, more=0):
            act.wait_ge(slab_in[n0 % 2], 16 * (n0 // 2 + 1) + 16 * i)
            if not (isinstance(i, int) and n0 + 2 * i < 2):
                act.wait_ge(mm_done, 2 * (n0 - 1) + more + 4 * i)
            act.activation(w_hi[n0 % 2][:], raw[n0 % 2][:], ACT.Copy).then_inc(hi_ready, 1)

        def split_lo(dve, n0, i):
            dve.wait_ge(hi_ready, n0 + 1 + 2 * i)
            dve.tensor_tensor(w_lo[n0 % 2][:], raw[n0 % 2][:], w_hi[n0 % 2][:].bitcast(F32),
                              ALU.subtract).then_inc(lo_ready, 1)

        def three_passes(pe, dst, wh, wl, xh, xl, first, last, **kw):
            pe.matmul(dst, wh, xh, start=first, stop=False, **kw)
            pe.matmul(dst, wh, xl, start=False, stop=False, **kw)
            return pe.matmul(dst, wl, xh, start=False, stop=last, **kw)

        def block_product(pe, dst, slot, j):
            wh, wl, c = by_cols(w_hi[slot]), by_cols(w_lo[slot]), slice(j * P, (j + 1) * P)
            for k in range(DB):
                mm = three_passes(pe, dst, wh[:, k, c], wl[:, k, c], h_hi[:, k, :], h_lo[:, k, :],
                                  k == 0, k == DB - 1)
            return mm

        def norm_squares(act, m, source, scale=None):
            for b in range(DB):
                src = source(act, b)
                if b >= 2 or m > 0:
                    act.wait_ge(sum_step, 7 * m + (max(1, b - 2) if b >= 2 else 0))
                act.activation(sq[:, b % 2, :], src, ACT.Square,
                               scale=1.0 if scale is None else scale(b)).then_inc(sq_ready, 1)

        def norm_rms(act, m):
            act.wait_ge(tot_ready, m + 1)
            act.activation(rms[:, :], bank[:, RB_BANK[m], 0:NCH], ACT.Sqrt, bias=eps[:, 0:1],
                           scale=1.0 / D).then_inc(rms_ready, 1)

        def norm_sum(dve, m, between=None):
            for b in range(1, DB):
                dve.wait_ge(sq_ready, 8 * m + b + 1)
                if b == 1:
                    dve.tensor_tensor(sum_sq[:, :], sq[:, 0, :], sq[:, 1, :], ALU.add).then_inc(sum_step, 1)
                else:
                    dve.wait_ge(sum_step, 7 * m + b - 1)
                    dve.tensor_tensor(sum_sq[:, :], sum_sq[:, :], sq[:, b % 2, :],
                                      ALU.add).then_inc(sum_step, 1)
            if between is not None:
                split_lo(dve, between, 0)
            dve.wait_ge(rms_ready, m + 1)
            dve.reciprocal(rrms[:, :], rms[:, :]).then_inc(rrms_ready, 1)

        def norm_total(pe, m):
            pe.wait_ge(sum_step, 7 * m + 7)
            for c in range(NCH):
                mm = pe.matmul(bank[:, RB_BANK[m], c:c + 1], sum_sq[:, c * P:(c + 1) * P], ones[:, 0:1],
                               start=True, stop=True)
            mm.then_inc(tot_ready, 1)

        def norm_spread(pe, m):
            pe.wait_ge(rrms_ready, m + 1)
            for c in range(NCH):
                mm = pe.matmul(bank[:, RB_BANK[m], c * P:(c + 1) * P], rrms[:, c:c + 1].to_broadcast([P, P]),
                               ident[:, :], start=True, stop=True)
            mm.then_inc(rb_ready, 1)

        def first_norm_act(act):
            def source(act, b):
                act.wait_ge(xres_ready, DB)
                return xres[:, b, :]
            norm_squares(act, 0, source)
            split_hi(act, S_DT, 0)
            norm_rms(act, 0)
            split_hi(act, S_BC, 0)
            for b in range(DB):
                act.wait_ge(hn_ready, b + 1)
                act.activation(h_hi[:, b, :], tmp[:, b % 2, :], ACT.Copy).then_inc(h_hi_ready, 1)

        def first_norm_dve(dve, weight):
            def low(b):
                dve.wait_ge(h_hi_ready, b + 1)
                dve.tensor_tensor(h_lo[:, b, :], tmp[:, b % 2, :], h_hi[:, b, :].bitcast(F32),
                                  ALU.subtract).then_inc(h_ready, 1)
            norm_sum(dve, 0, S_DT)
            split_lo(dve, S_BC, 0)
            dve.wait_ge(rb_ready, 1)
            for b in range(DB):
                if b >= 2:
                    dve.wait_ge(h_ready, b - 1)
                dve.scalar_tensor_tensor(tmp[:, b % 2, :], xres[:, b, :], weight(b), bank[:, 0, :],
                                         ALU.mult, ALU.mult).then_inc(hn_ready, 1)
                if b >= 1:
                    low(b - 1)
            low(DB - 1)

        def boundary_act(act, u, ready, scale=None, more=None, last=False):
            m = 2 * u + 1
            act.wait_ge(*ready(0))
            act.activation(tmp[:, 3, :], bank[:, 0, :], ACT.Copy).then_inc(f0_ready, 1)

            def source(act, b):
                act.wait_ge(*ready(b))
                return bank[:, b, :]
            norm_squares(act, m, source, scale)
            norm_rms(act, m)
            if more is not None:
                split_hi(act, more[0], 0, more[1])
            if last:
                return
            for i, b in enumerate(ORDER):
                act.wait_ge(hn_ready, DB * (u + 1) + i + 1)
                act.activation(h_hi[:, b, :], tmp[:, 2 + i % 2, :], ACT.Copy).then_inc(h_hi_ready, 1)
            norm_squares(act, m + 1, lambda act, b: xres[:, b, :])
            norm_rms(act, m + 1)

        def boundary_dve(dve, u, post, pre=None, more=None):
            m = 2 * u + 1

            def renew(i):
                b = ORDER[i]
                if i >= 2:
                    dve.wait_ge(x_updated, DB * u + i - 1)
                dve.scalar_tensor_tensor(tmp[:, i % 2, :], bank[:, b, :] if b else tmp[:, 3, :], post(b),
                                         rrms_all[:, :], ALU.mult, ALU.mult).then_inc(post_step, 1)
                dve.wait_ge(post_step, DB * u + i + 1)
                dve.tensor_tensor(xres[:, b, :], xres[:, b, :], tmp[:, i % 2, :], ALU.add).then_inc(x_updated, 1)

            def weighted(i):
                b = ORDER[i]
                dve.wait_ge(x_updated, DB * u + max(i, 1 if i < 2 else i) + 1)
                if i >= 2:
                    dve.wait_ge(h_ready, DB * (u + 1) + i - 1)
                dve.tensor_scalar(tmp[:, 2 + i % 2, :], xres[:, b, :], pre(b), None, ALU.mult).then_inc(hn_ready, 1)

            def low(i):
                b = ORDER[i]
                dve.wait_ge(h_hi_ready, DB * (u + 1) + i + 1)
                dve.tensor_tensor(h_lo[:, b, :], tmp[:, 2 + i % 2, :], h_hi[:, b, :].bitcast(F32),
                                  ALU.subtract).then_inc(h_ready, 1)

            norm_sum(dve, m)
            if more is not None:
                split_lo(dve, more, 0)
            dve.wait_ge(f0_ready, u + 1)
            dve.wait_ge(rb_ready, m + 1)
            dve.tensor_copy(rrms_all[:, :], bank[:, 0, :]).then_inc(rb_copied, 1)
            dve.wait_ge(rb_copied, m if u else 1)
            for i in range(5):
                renew(i)
            if pre is None:
                for i in range(5, DB):
                    renew(i)
                return
            weighted(0)
            for i in range(1, DB):
                if i >= 5:
                    renew(i)
                weighted(i)
                low(i - 1)
            low(DB - 1)
            norm_sum(dve, m + 1)
            dve.wait_ge(rb_ready, m + 2)
            dve.tensor_copy(rrms_all[:, :], bank[:, RB_BANK[m + 1], :]).then_inc(rb_copied, 1)
            dve.wait_ge(rb_copied, m + 1)

        RB_BANK = [0, 0, 0, 0, 2, 0, 0, 0]

        def last_tap(act, block, slot, w, b):
            act.activation(tmp[:, slot, :], bank[:, 4 + slot, :], ACT.Identity, bias=b,
                           scale=w).then_inc(conv_tap, 1)

        def other_taps(dve, count, part, slot, weights):
            dve.wait_ge(conv_tap, count + 1)
            n = len(weights)
            for j, w in enumerate(weights):
                back = j + 1
                if j:
                    dve.wait_ge(conv_part, part + j)
                dve.scalar_tensor_tensor(tmp[:, slot, back:], bank[:, 4 + slot, 0:T - back], w,
                                         tmp[:, slot, back:], ALU.mult, ALU.add
                                         ).then_inc(conv_part if j < n - 1 else conv_done, 1)

        def xbc_pe(pe, n0, i, it):
            for s in range(2):
                pe.wait_ge(lo_ready, n0 + s + 1 + 2 * i)
                for j in range(2):
                    q = 2 * s + j
                    if not isinstance(it, int) or it > 0:
                        pe.wait_ge(conv_done, 4 * it + q - 3)
                    block_product(pe, bank[:, 4 + q, :], (n0 + s) % 2, j).then_inc(mm_done, 1)

        def xbc_act(act, n0, i, it, blk, split=True):
            def finish(q):
                act.wait_ge(conv_done, 4 * it + q + 1)
                act.activation(xbc[:, blk + q, :], tmp[:, q, :], ACT.Silu).then_inc(conv_silu, 1)
            for s in range(2):
                if s or split:
                    split_hi(act, n0 + s + 1, i)
                for j in range(2):
                    q = 2 * s + j
                    act.wait_ge(mm_done, 2 * (n0 + s) + j + 1 + 4 * i)
                    if not isinstance(it, int) or it > 0:
                        act.wait_ge(conv_silu, 4 * it + q - 3)
                    last_tap(act, None, q, col("conv_w", (SSD_TAPS - 1) * CB + blk + q), col("conv_b", blk + q))
                    if q:
                        finish(q - 1)
            finish(3)

        def xbc_dve(dve, n0, i, it, blk, split=True):
            for s in range(2):
                if s or split:
                    split_lo(dve, n0 + s + 1, i)
                for j in range(2):
                    q = 2 * s + j
                    other_taps(dve, 4 * it + q, 2 * (4 * it + q), q,
                               [col("conv_w", t * CB + blk + q) for t in reversed(range(SSD_TAPS - 1))])

        def small(ap):
            return ap.rearrange("p (c h) -> p c h", h=HEADS)

        DT_STEPS = 16

        def dt_feat_act(act):
            act.wait_ge(mm_done, 2)
            act.activation(gate[0:HEADS, 0, :], bank[0:HEADS, 1, :], ACT.Copy).then_inc(dt_feat_ready, 1)

        def dt_chain_act(act):
            act.wait_ge(sel_made, 1)
            act.activation(sel[:], decay[0:HPG, :, :].rearrange("r a (b n) -> r (a b) n", n=P),
                           ACT.Copy).then_inc(sel_ready, 1)
            act.wait_ge(heads_loaded, 48)
            act.activation(neg_a[:, :], heads_in[:, 1, :], ACT.Exp).then_inc(dt_act, 1)
            act.wait_ge(dt_vec, 1)
            act.activation(e_dt[:], v_dt[:], ACT.Abs).then_inc(dt_act, 1)
            act.wait_ge(dt_act, 2)
            act.activation(e_dt[:], e_dt[:], ACT.Exp, scale=-1.0).then_inc(dt_act, 1)
            act.wait_ge(dt_vec, 2)
            act.activation(l_dt[:], u_dt[:], ACT.Ln).then_inc(dt_act, 1)

        def dt_decays_act(act):
            act.wait_ge(cum_ready, 1)
            act.activation(a_cum[:], small(bank[:, 2, 0:NCH * HEADS]), ACT.Copy).then_inc(dt_act, 1)
            act.activation(chunk_decay[:], small(bank[:, 3, 0:NCH * HEADS]), ACT.Exp).then_inc(dt_act, 1)
            act.wait_ge(dt_vec, DT_STEPS)
            act.activation(to_end[:], to_end[:], ACT.Exp).then_inc(dt_act, 1)

        def dt_chain_dve(dve):
            n = [0]

            def step(ins):
                n[0] += 1
                ins.then_inc(dt_vec, 1)
                dve.wait_ge(dt_vec, n[0])

            def over_chunks(row):
                return row.unsqueeze(1).to_broadcast([P, NCH, HEADS])

            dve.wait_ge(heads_loaded, 48)
            dve.wait_ge(dt_T, 1)
            step(dve.tensor_tensor(v_dt[:], small(bank[:, 1, 0:NCH * HEADS]), over_chunks(heads_in[:, 0, :]),
                                   ALU.add))
            dve.wait_ge(dt_act, 3)
            step(dve.tensor_scalar(u_dt[:], e_dt[:], 1.0, None, ALU.add))
            step(dve.tensor_scalar(d_dt[:], u_dt[:], -1.0, None, ALU.add))
            step(dve.tensor_scalar(z_dt[:], d_dt[:], 0.0, None, ALU.is_equal))
            step(dve.tensor_tensor(d_dt[:], d_dt[:], z_dt[:], ALU.add))
            step(dve.reciprocal(d_dt[:], d_dt[:]))
            step(dve.tensor_tensor(d_dt[:], d_dt[:], e_dt[:], ALU.mult))
            dve.wait_ge(dt_act, 4)
            step(dve.tensor_tensor(l_dt[:], l_dt[:], z_dt[:], ALU.add))
            step(dve.tensor_tensor(d_dt[:], d_dt[:], l_dt[:], ALU.mult))
            step(dve.tensor_scalar(v_dt[:], v_dt[:], 0.0, None, ALU.max))
            step(dve.tensor_tensor(dt[:], v_dt[:], d_dt[:], ALU.add))
            step(dve.tensor_scalar(neg_a[:, :], neg_a[:, :], -1.0, None, ALU.mult))
            step(dve.tensor_tensor(a_dt[:], dt[:], over_chunks(neg_a[:, :]), ALU.mult))
            pairs = heads_in[:, 2, :].rearrange("p (j h) -> p j h", h=2)
            step(dve.tensor_copy(d_pair[0:HD, :], pairs[0:HD, :, 0]))
            step(dve.tensor_copy(d_pair[HD:P, :], pairs[HD:P, :, 1]))
            assert n[0] == DT_STEPS - 1

        def dt_to_end_dve(dve):
            dve.wait_ge(dt_act, 6)
            dve.tensor_tensor(to_end[:], small(bank[:, 3, 0:NCH * HEADS]), a_cum[:],
                              ALU.subtract).then_inc(dt_vec, 1)

        def dt_product_pe(pe):
            pe.wait_ge(lo_ready, S_DT + 1)
            wh, wl = by_cols(w_hi[0]), by_cols(w_lo[0])
            for k in range(DB):
                pe.wait_ge(h_ready, k + 1)
                mm = three_passes(pe, bank[:, 1, :], wh[:, k, 0:P], wl[:, k, 0:P], h_hi[:, k, :], h_lo[:, k, :],
                                  k == 0, k == DB - 1)
                if k % 4 == 3:
                    mm.then_inc(mm_done, 1)

        def dt_transpose_pe(pe):
            pe.wait_ge(dt_feat_ready, 1)
            for c in range(NCH):
                mm = pe.transpose(bank[:, 1, c * HEADS:(c + 1) * HEADS], gate[0:HEADS, 0, c * P:(c + 1) * P],
                                  ident[0:HEADS, 0:HEADS])
            mm.then_inc(dt_T, 1)

        def dt_sums_pe(pe):
            pe.wait_ge(dt_vec, 13)
            rhs = a_dt[:].rearrange("p c h -> p (c h)")
            pe.matmul(bank[:, 2, 0:NCH * HEADS], upper[:], rhs, start=True, stop=True)
            pe.matmul(bank[:, 3, 0:NCH * HEADS], ones[:], rhs, start=True, stop=True).then_inc(cum_ready, 1)

        def cs(c):
            return slice(c * P, (c + 1) * P)

        def group_feat(block, ap=slice(None)):
            return xbc[:, bass.ds(block, 1), ap].rearrange("p a l -> p (a l)")

        def used_before(p, per=1):
            return max(1, 1 + per * (p - 1)) if isinstance(p, int) else 1 + per * (p - 1)

        def decay_slot(q, h):
            return decay[:, h, :] if q % 2 == 0 else tmp[:, 2 + h, :]

        def scan_pe(pe, g, opening=False, last=False):
            def front(g, q):
                p = QPG * g + q
                pe.wait_ge(x_feat_ready, p + 1)
                pe.wait_ge(xdt_ready, 1 + p)
                for c in range(NCH):
                    mm = pe.transpose(bank[:, 1, cs(c)], x_feat[:, cs(c)], ident[:])
                mm.then_inc(x_tok_mm, 1)
                if q == 0:
                    pe.wait_ge(ac_ready, g + 1)
                for h in range(2):
                    pe.wait_ge(diff_ready, 1 + 2 * p)
                    pe.matmul(bank[:, 2 + h, :], sel[:, 2 * q + h, :], ac_hi[:, :], start=True, stop=False)
                    pe.matmul(bank[:, 2 + h, :], sel[:, 2 * q + h, :], ac_lo[:, :], start=False,
                              stop=True).then_inc(r_mm, 1)
                pe.wait_ge(fs_ready, 1 + p)
                pair = sel[:].rearrange("r b n -> r (b n)")[:, 2 * q * P + HD:2 * q * P + HD + P]
                pe.matmul(bank[:, 5, :], pair, ac_hi[:, :], start=True, stop=False)
                pe.matmul(bank[:, 5, :], pair, ac_lo[:, :], start=False, stop=True).then_inc(fs_mm, 1)

            def z_block(g, q):
                n = S_Z + q // 2
                if q % 2 == 0:
                    pe.wait_ge(lo_ready, n + 1 + 2 * g)
                pe.wait_ge(gate_ready, 1 + QPG * g + q)
                block_product(pe, bank[:, 0, :], n % 2, q % 2).then_inc(mm_done, 1)

            def open_group(g):
                if opening:
                    z_block(g, 0)
                    pe.wait_ge(conv_done, CB)
                pe.wait_ge(a_dt_g_ready, g + 1)
                pe.wait_ge(fs_ready, 1 + QPG * g)
                for c in range(NCH):
                    mm = pe.matmul(bank[0:HPG, 5, cs(c)], a_dt_g[:, c, :], upper[:], start=True, stop=True)
                mm.then_inc(acg_mm, 1)
                if not opening:
                    z_block(g, 0)
                pe.wait_ge(b_feat_ready, g + 1)
                pe.wait_ge(st_step, 1 + 20 * g)
                for c in range(NCH):
                    mm = pe.transpose(bank[:, 4, cs(c)], b_feat[:, cs(c)], ident[:])
                mm.then_inc(b_tok_mm, 1)
                front(g, 0)

            if opening:
                open_group(g)
                return
            for q in range(QPG):
                p = QPG * g + q
                if q == 0:
                    pe.wait_ge(b_tok_ready, g + 1)
                pe.wait_ge(xdt_end_ready, p + 1)
                for c in range(NCH - 1):
                    mm = pe.matmul(bank[:, 4, cs(c)], b_tok[:, cs(c)], xdt_end[:, cs(c)], start=True, stop=True)
                mm.then_inc(st_mm, 1)
                if q < QPG - 1:
                    front(g, q + 1)
                elif not last:
                    open_group(g + 1)
                if q == 0:
                    pe.wait_ge(y_step, 1 + 12 * g)
                    for c in range(NCH):
                        mm = pe.matmul(bank[:, 6, cs(c)], b_feat[:, cs(c)], group_feat(IB + G + g, cs(c)),
                                       start=True, stop=True)
                    mm.then_inc(cb_mm, 1)
                if q == 1:
                    pe.wait_ge(gate_ready, 1 + p + 1)
                    pe.wait_ge(gsum_step, 1 + 3 * g)
                    for c in range(NCH):
                        mm = pe.matmul(bank[:, 0, c:c + 1], sum_sq[:, cs(c)], ones[:, 0:1], start=True, stop=True)
                    mm.then_inc(gtot_mm, 1)
                    pe.wait_ge(gtot_ready, g + 1)
                if q < QPG - 1:
                    z_block(g, q + 1)
                pe.wait_ge(y_step, 1 + 3 * p - (1 if q else 0))
                pe.wait_ge(cb_ready, g + 1)
                pe.wait_ge(st_step, 1 + 5 * p + 5)
                for c in range(1, NCH):
                    mm = pe.matmul(bank[:, 6, cs(c)], state[:, c - 1, :], group_feat(IB + G + g, cs(c)),
                                   start=True, stop=True)
                mm.then_inc(yo_mm, 1)
                for h in range(2):
                    pe.wait_ge(m_ready, 2 * p + h + 1)
                    for c in range(NCH):
                        mm = pe.matmul(bank[h * HD:(h + 1) * HD, 7, cs(c)],
                                       xdt[:, q % 2, c * P + h * HD:c * P + (h + 1) * HD],
                                       decay_slot(q, h)[:, cs(c)], start=True, stop=True)
                mm.then_inc(yd_mm, 1)

        def scan_act(act, g, opening=False, last=False):
            def x_copy(g, q):
                act.wait_ge(x_tok_mm, 1 + QPG * g + q)
                act.activation(x_feat[:, :], group_feat(QPG * g + q), ACT.Copy).then_inc(x_feat_ready, 1)

            def exps(g, q):
                p = QPG * g + q
                for h in range(2):
                    act.wait_ge(diff_ready, 1 + 2 * p + h + 1)
                    act.activation(decay_slot(q, h), decay_slot(q, h), ACT.Relu).then_inc(relu_ready, 1)
                for h in range(2):
                    act.wait_ge(relu_ready, 2 * p + h + 1)
                    act.activation(decay_slot(q, h), decay_slot(q, h), ACT.Exp, scale=-1.0).then_inc(exp_ready, 1)
                act.wait_ge(fs_mm, 1 + p + 1)
                act.wait_ge(y_step, used_before(p, 3))
                act.activation(from_start[:, q % 2, :], bank[:, 5, :], ACT.Exp).then_inc(fs_ready, 1)

            def square(q):
                p = QPG * g + q
                act.wait_ge(y_done, 1 + p + 1)
                act.wait_ge(gsum_step, 1 + 3 * g + max(0, q - 2))
                act.sem_inc(y_seen, 1)
                act.activation(sq[:, q % 2, :], group_feat(p), ACT.Square).then_inc(ysq_ready, 1)

            def gate_of(g, q):
                p = QPG * g + q
                act.wait_ge(mm_done, 2 * (S_Z + q // 2) + q % 2 + 1 + 4 * g)
                act.wait_ge(y_done, used_before(p))
                act.activation(gate[:, q % 2, :], bank[:, 0, :], ACT.Silu).then_inc(gate_ready, 1)

            def open_inputs(g):
                act.wait_ge(acg_mm, 1 + g)
                act.activation(a_dt_g[:], a_dt[:, :, bass.ds(HPG * g, HPG)], ACT.Copy).then_inc(a_dt_g_ready, 1)
                act.wait_ge(cb_mm, 1 + g)
                act.activation(b_feat[:, :], group_feat(IB + g), ACT.Copy).then_inc(b_feat_ready, 1)

            def open_group(g):
                act.wait_ge(acg_mm, 1 + g + 1)
                act.wait_ge(fs_mm, 1 + QPG * g)
                act.activation(ac_hi[:, :], bank[0:HPG, 5, :], ACT.Copy).then_inc(ac_hi_ready, 1)
                gate_of(g, 0)
                act.wait_ge(b_tok_mm, g + 1)
                act.wait_ge(st_mm, 1 + QPG * g)
                act.activation(b_tok[:, :], bank[:, 4, :], ACT.Copy).then_inc(b_tok_ready, 1)
                x_copy(g, 1)
                exps(g, 0)

            if opening:
                open_inputs(g)
                x_copy(g, 0)
                open_group(g)
                return
            for q in range(QPG):
                p = QPG * g + q
                if q >= 1:
                    square(q - 1)
                if q == 1:
                    act.wait_ge(gtot_mm, 1 + g + 1)
                    act.activation(group_ms[:, bass.ds(g, 1), :].rearrange("p a c -> p (a c)"),
                                   bank[:, 0, 0:NCH], ACT.Copy).then_inc(gtot_ready, 1)
                if q == 0:
                    split_hi(act, S_Z + 1, g)
                if q == 2:
                    split_hi(act, S_Z + 2, g)
                if q == 2 and not last:
                    open_inputs(g + 1)
                if q < QPG - 1:
                    exps(g, q + 1)
                    if q < QPG - 2:
                        x_copy(g, q + 2)
                    elif not last:
                        x_copy(g + 1, 0)
                    gate_of(g, q + 1)
                elif not last:
                    open_group(g + 1)
            square(QPG - 1)

        def scan_dve(dve, g, opening=False, last=False):
            def by_head(ap):
                return ap.rearrange("p (c h d) -> p c h d", h=2, d=HD)

            def front(g, q):
                p = QPG * g + q

                def heads(table):
                    return table[:, :, bass.ds(HPG * g + 2 * q, 2)].unsqueeze(3).to_broadcast([P, NCH, 2, HD])
                dve.wait_ge(x_tok_mm, 1 + p + 1)
                dve.wait_ge(yd_mm, used_before(p))
                dve.tensor_tensor(by_head(xdt[:, q % 2, :]), by_head(bank[:, 1, :]), heads(dt),
                                  ALU.mult).then_inc(xdt_ready, 1)
                for h in range(2):
                    dve.wait_ge(r_mm, 2 * p + h + 1)
                    dve.tensor_tensor(chunked(decay_slot(q, h)),
                                      a_cum[:, :, bass.ds(HPG * g + 2 * q + h, 1)].to_broadcast([P, NCH, P]),
                                      chunked(bank[:, 2 + h, :]), ALU.subtract).then_inc(diff_ready, 1)
                dve.wait_ge(xdt_ready, 1 + p + 1)
                dve.wait_ge(st_mm, 1 + p)
                dve.tensor_tensor(by_head(xdt_end[:, :]), by_head(xdt[:, q % 2, :]), heads(to_end),
                                  ALU.mult).then_inc(xdt_end_ready, 1)

            def states(g, q):
                p = QPG * g + q
                dve.wait_ge(st_mm, 1 + p + 1)
                dve.wait_ge(yo_mm, 1 + p)
                dve.tensor_copy(state[:, 0, :], bank[:, 4, 0:P]).then_inc(st_step, 1)
                for c in range(1, NCH - 1):
                    dve.wait_ge(st_step, 1 + 5 * p + 2 * c - 1)
                    dve.tensor_tensor(state[:, c, :].rearrange("p (h d) -> p h d", d=HD),
                                      state[:, c - 1, :].rearrange("p (h d) -> p h d", d=HD),
                                      chunk_decay[:, c, bass.ds(HPG * g + 2 * q, 2)].unsqueeze(2).to_broadcast(
                                          [P, 2, HD]), ALU.mult).then_inc(st_step, 1)
                    dve.wait_ge(st_step, 1 + 5 * p + 2 * c)
                    dve.tensor_tensor(state[:, c, :], state[:, c, :], bank[:, 4, cs(c)],
                                      ALU.add).then_inc(st_step, 1)

            def group_sum(q):
                p = QPG * g + q
                dve.wait_ge(ysq_ready, p + 1)
                if q == 1:
                    dve.tensor_tensor(sum_sq[:, :], sq[:, 0, :], sq[:, 1, :], ALU.add).then_inc(gsum_step, 1)
                elif q > 1:
                    dve.wait_ge(gsum_step, 1 + 3 * g + q - 1)
                    dve.tensor_tensor(sum_sq[:, :], sum_sq[:, :], sq[:, q % 2, :], ALU.add).then_inc(gsum_step, 1)

            def open_group(g):
                dve.wait_ge(ac_hi_ready, g + 1)
                dve.tensor_tensor(ac_lo[:, :], bank[0:HPG, 5, :], ac_hi[:, :].bitcast(F32),
                                  ALU.subtract).then_inc(ac_ready, 1)
                front(g, 0)

            if opening:
                open_group(g)
                states(g, 0)
                return
            for q in range(QPG):
                p = QPG * g + q
                if q == 0:
                    dve.wait_ge(cb_mm, 1 + g + 1)
                    dve.tensor_tensor(chunked(cb_mask[:, :]), chunked(bank[:, 6, :]),
                                      upper[:].unsqueeze(1).to_broadcast([P, NCH, P]), ALU.mult).then_inc(cb_ready, 1)
                    dve.wait_ge(cb_ready, g + 1)
                else:
                    states(g, q)
                for h in range(2):
                    dve.wait_ge(exp_ready, 2 * p + h + 1)
                    dve.tensor_tensor(decay_slot(q, h), decay_slot(q, h), cb_mask[:, :],
                                      ALU.mult).then_inc(m_ready, 1)
                if q < QPG - 1:
                    front(g, q + 1)
                elif not last:
                    open_group(g + 1)
                if q == 0:
                    split_lo(dve, S_Z + 1, g)
                if q == 2:
                    split_lo(dve, S_Z + 2, g)
                if q >= 1:
                    group_sum(q - 1)
                x_p = group_feat(p)
                dve.wait_ge(fs_ready, 1 + p + 1)
                dve.wait_ge(yo_mm, 1 + p + 1)
                dve.tensor_tensor(tmp[:, 1, P:], bank[:, 6, P:], from_start[:, q % 2, P:], ALU.mult).then_inc(y_step, 1)
                dve.wait_ge(yd_mm, 1 + p + 1)
                dve.scalar_tensor_tensor(tmp[:, 0, :], x_p, d_pair[:, bass.ds(p, 1)], bank[:, 7, :],
                                         ALU.mult, ALU.add).then_inc(y_step, 1)
                dve.wait_ge(y_step, 1 + 3 * p + 2)
                dve.tensor_tensor(tmp[:, 0, P:], tmp[:, 0, P:], tmp[:, 1, P:], ALU.add).then_inc(y_step, 1)
                dve.wait_ge(y_step, 1 + 3 * p + 3)
                dve.wait_ge(gate_ready, 1 + p + 1)
                dve.tensor_tensor(x_p, tmp[:, 0, :], gate[:, q % 2, :], ALU.mult).then_inc(y_done, 1)
            if not last:
                states(g + 1, 0)
            group_sum(QPG - 1)

        def group_norm_act(act):
            act.wait_ge(gtot_mm, 1 + G + 1)
            act.activation(group_ms[:, G, :], bank[:, 0, 0:NCH], ACT.Copy).then_inc(gtot_ready, 1)
            act.wait_ge(gtot_ready, G + 1)
            act.activation(group_ms[:], group_ms[:], ACT.Sqrt, bias=eps[:, 0:1],
                           scale=1.0 / (D_INNER // G)).then_inc(grms_ready, 1)

        def group_scale_act(act, g):
            act.wait_ge(grb_mm, g + 1)
            act.activation(group_scale[:, g, :], bank[:, 4 + g, :], ACT.Copy).then_inc(group_scale_ready, 1)

        def group_norm_dve(dve):
            dve.wait_ge(grms_ready, 1)
            dve.reciprocal(group_ms[:], group_ms[:]).then_inc(grrms_ready, 1)

        def group_norm_pe(pe):
            pe.wait_ge(gate_ready, 1 + IB)
            pe.wait_ge(gsum_step, 1 + 3 * G)
            for c in range(NCH):
                mm = pe.matmul(bank[:, 0, c:c + 1], sum_sq[:, cs(c)], ones[:, 0:1], start=True, stop=True)
            mm.then_inc(gtot_mm, 1)
            pe.wait_ge(grrms_ready, 1)
            for g in range(G):
                for c in range(NCH):
                    mm = pe.matmul(bank[:, 4 + g, cs(c)], group_ms[:, g + 1, c:c + 1].to_broadcast([P, P]), ident[:],
                                   start=True, stop=True)
                mm.then_inc(grb_mm, 1)

        def y_split_act(act, n0, i, blk):
            for k in range(2):
                act.wait_ge(yn_ready, blk + k + 1)
                if not (isinstance(i, int) and n0 + 2 * i < S_OUT + 2):
                    act.wait_ge(mm_done, 2 * (n0 - 1) + 4 * i)
                act.activation(y_hi[n0 % 2][:, k, :], tmp[:, 2 * (n0 % 2) + k, :], ACT.Copy).then_inc(y_hi_ready, 1)

        def y_split_dve(dve, n0, i, blk, g):
            for k in range(2):
                s = 2 * (n0 % 2) + k
                if isinstance(blk, int):
                    y_b, scale = xbc[:, blk + k, :], group_scale[:, g, :]
                else:
                    y_b = xbc[:, bass.ds(blk + k, 1), :].rearrange("p a l -> p (a l)")
                    scale = group_scale[:, bass.ds(g, 1), :].rearrange("p a l -> p (a l)")
                dve.scalar_tensor_tensor(tmp[:, s, :], y_b, col("ssd_norm", blk + k), scale, ALU.mult,
                                         ALU.mult).then_inc(yn_ready, 1)
            for k in range(2):
                s = 2 * (n0 % 2) + k
                dve.wait_ge(y_hi_ready, blk + k + 1)
                dve.tensor_tensor(y_lo[n0 % 2][:, k, :], tmp[:, s, :], y_hi[n0 % 2][:, k, :].bitcast(F32),
                                  ALU.subtract).then_inc(y_ready, 1)

        def rows_product(pe, slot, xs, first=False, last=False, banks_read=None):
            wh, wl = by_rows(w_hi[slot]), by_rows(w_lo[slot])
            for b in range(DB):
                if b == 4 and banks_read is not None:
                    pe.wait_ge(*banks_read)
                for k, (xh, xl) in enumerate(xs):
                    mm = three_passes(pe, bank[:, b, :], wh[:, k, b * P:(b + 1) * P], wl[:, k, b * P:(b + 1) * P],
                                      xh, xl, first and k == 0, last and k == 1)
                if last or b % 4 == 3:
                    mm.then_inc(mm_done, 1)

        def out_pe(pe, n0, i, blk, first=False, last=False):
            pe.wait_ge(lo_ready, n0 + 1 + 2 * i)
            pe.wait_ge(y_ready, blk + 2)
            rows_product(pe, n0 % 2, [(y_hi[n0 % 2][:, k, :], y_lo[n0 % 2][:, k, :]) for k in range(2)],
                         first, last, (group_scale_ready, G) if first else None)

        CONV0 = [CB, CB + 2 * FB]
        PART0 = [2 * CB, 2 * CB + 2 * FB]

        def up_first_pe(pe, l):
            pe.wait_ge(lo_ready, S_UP[l] + 2)
            for i, k in enumerate(ORDER):
                pe.wait_ge(h_ready, DB * (2 * l + 1) + i + 1)
                for q in range(4):
                    slot, c = (S_UP[l] + q // 2) % 2, slice((q % 2) * P, (q % 2 + 1) * P)
                    mm = three_passes(pe, bank[:, 4 + q, :], by_cols(w_hi[slot])[:, k, c],
                                      by_cols(w_lo[slot])[:, k, c], h_hi[:, k, :], h_lo[:, k, :],
                                      i == 0, i == DB - 1)
                    if i == DB - 1:
                        mm.then_inc(mm_done, 1)
            norm_total(pe, 4 * l + 2)
            norm_spread(pe, 4 * l + 2)

        def up_pe(pe, l, i):
            for s in range(2):
                pe.wait_ge(lo_ready, S_UP[l] + s + 1 + 2 * i)
                for j in range(2):
                    q = 2 * s + j
                    pe.wait_ge(conv_done, CONV0[l] + q - 3 + 4 * i)
                    block_product(pe, bank[:, 4 + q, :], (S_UP[l] + s) % 2, j).then_inc(mm_done, 1)

        def up_act(act, l, i, split=True):
            for s in range(2):
                if s or split:
                    split_hi(act, S_UP[l] + s + 1, i, MORE_UP[l])
                for j in range(2):
                    q, blk = 2 * s + j, s * FB + j
                    act.wait_ge(scaled, CONV0[l] - CB + q + 1 + 4 * i)
                    if s == 0:
                        act.wait_ge(u_ready, 1 + FB * l + 2 * i)
                    else:
                        act.wait_ge(act_ready, 1 + FB * l + 2 * i)
                    last_tap(act, None, q, col("ffn_w", (l * FFN_TAPS + FFN_TAPS - 1) * 2 * FB + blk + 2 * i),
                             col("ffn_b", l * 2 * FB + blk + 2 * i))
                if s == 0:
                    for j in range(2):
                        act.wait_ge(conv_done, CONV0[l] + j + 1 + 4 * i)
                        act.activation(tmp[:, j, :], tmp[:, j, :], ACT.Silu).then_inc(gate_silu, 1)
            for j in range(2):
                act.wait_ge(u_ready, 1 + FB * l + j + 1 + 2 * i)
                act.activation(act_hi[:, bass.ds(2 * i + j, 1), :].rearrange("p a l -> p (a l)"),
                               tmp[:, 2 + j, :], ACT.Copy).then_inc(act_hi_ready, 1)

        def up_dve(dve, l, i, split=True):
            for s in range(2):
                if s or split:
                    split_lo(dve, S_UP[l] + s + 1, i)
                for j in range(2):
                    q = 2 * s + j
                    dve.wait_ge(mm_done, 2 * (S_UP[l] + s) + MORE_UP[l] + j + 1 + 4 * i)
                    dve.tensor_tensor(bank[:, 4 + q, :], bank[:, 4 + q, :], rrms_all[:, :],
                                      ALU.mult).then_inc(scaled, 1)
                for j in range(2):
                    q, blk = 2 * s + j, s * FB + j
                    other_taps(dve, CONV0[l] + q + 4 * i, PART0[l] + q + 4 * i, q,
                               [col("ffn_w", (l * FFN_TAPS + t) * 2 * FB + blk + 2 * i)
                                for t in reversed(range(FFN_TAPS - 1))])
            for j in range(2):
                dve.wait_ge(gate_silu, FB * l + j + 1 + 2 * i)
                dve.wait_ge(conv_done, CONV0[l] + 2 + j + 1 + 4 * i)
                dve.tensor_tensor(tmp[:, 2 + j, :], tmp[:, j, :], tmp[:, 2 + j, :], ALU.mult).then_inc(u_ready, 1)
            for j in range(2):
                blk = bass.ds(2 * i + j, 1)
                dve.wait_ge(act_hi_ready, FB * l + j + 1 + 2 * i)
                dve.tensor_tensor(act_lo[:, blk, :].rearrange("p a l -> p (a l)"), tmp[:, 2 + j, :],
                                  act_hi[:, blk, :].rearrange("p a l -> p (a l)").bitcast(F32),
                                  ALU.subtract).then_inc(act_ready, 1)

        def down_pe(pe, l, s0, i, first=False, last=False):
            n0 = S_DOWN[l] + s0
            pe.wait_ge(lo_ready, n0 + 1 + 2 * i)
            pe.wait_ge(act_ready, 1 + FB * l + 2 * s0 + 2 + 4 * i)
            if isinstance(i, int):
                xs = [(act_hi[:, 2 * s0 + k, :], act_lo[:, 2 * s0 + k, :]) for k in range(2)]
            else:
                xs = [(act_hi[:, bass.ds(2 * s0 + k + 4 * i, 1), :].rearrange("p a l -> p (a l)"),
                       act_lo[:, bass.ds(2 * s0 + k + 4 * i, 1), :].rearrange("p a l -> p (a l)"))
                      for k in range(2)]
            rows_product(pe, n0 % 2, xs, first, last, (conv_done, CONV0[l] + 2 * FB) if first else None)

        POOL_ORDER = [4, 5, 6, 7, 0, 1, 2, 3]
        PAD = max(POOL_WINDOWS)
        WIN_STEPS = [0]
        for b in POOL_ORDER:
            WIN_STEPS.append(WIN_STEPS[-1] + 2 + POOL_WINDOWS[b // 2].bit_length() - 1)

        def pool_pe(pe):
            pe.wait_ge(lo_ready, S_POOL + 1)
            wh, wl = (t[S_POOL % 2][:].rearrange("p (g k n) -> p g k n", g=G, k=2) for t in (w_hi, w_lo))
            for b in POOL_ORDER:
                g, c = b // 2, slice((b % 2) * P, (b % 2 + 1) * P)
                if b == 2:
                    norm_total(pe, 4)
                    norm_spread(pe, 4)
                    pe.wait_ge(rb_copied, 4)
                pe.wait_ge(h_ready, 2 * DB + 1 + max(ORDER.index(2 * g), ORDER.index(2 * g + 1)))
                for k in range(2):
                    mm = three_passes(pe, bank[:, b, :], wh[:, g, k, c], wl[:, g, k, c], h_hi[:, 2 * g + k, :],
                                      h_lo[:, 2 * g + k, :], k == 0, k == 1)
                mm.then_inc(mm_done, 1)

        def pool_dve(dve):
            dve.wait_ge(pads_zero, 1)
            for i, b in enumerate(POOL_ORDER):
                n, w = WIN_STEPS[i], POOL_WINDOWS[b // 2]
                dve.wait_ge(mm_done, 2 * S_POOL + MORE_POOL + i + 1)
                if i:
                    dve.wait_ge(mixed, i)
                dve.tensor_tensor(win[:, 0, PAD:], bank[:, b, :], rrms_all[:, :], ALU.mult).then_inc(win_step, 1)
                src, back = 0, 1
                while back < w:
                    n += 1
                    dve.wait_ge(win_step, n)
                    dst = 1 if src != 1 else 2
                    dve.tensor_tensor(win[:, dst, PAD:], win[:, src, PAD:], win[:, src, PAD - back:PAD + T - back],
                                      ALU.add).then_inc(win_step, 1)
                    src, back = dst, 2 * back
                n += 1
                dve.wait_ge(win_step, n)
                dve.tensor_tensor(win[:, src, PAD:2 * PAD], win[:, src, PAD:2 * PAD], edge[:, b // 2, :],
                                  ALU.mult).then_inc(win_step, 1)
                n += 1
                assert n == WIN_STEPS[i + 1]
                dve.wait_ge(win_step, n)
                dve.scalar_tensor_tensor(bank[:, b, :], win[:, src, PAD:], 1.0 / w, win[:, 0, PAD:], ALU.mult,
                                         ALU.subtract).then_inc(mixed, 1)

        def norm_col(name, l):
            return lambda b: col(name, l * DB + b)

        block = ctx.enter_context(nc.Block())

        @block.sync
        def _(sp):
            sp.dma_start(x_rows[:], x[0].rearrange("(c p) d -> p c d", p=P)).then_inc(x_in, 16)
            sp.wait_ge(consts, 1)
            for t, r, n, src in par_pieces:
                sp.dma_start(par_rows[r:r + n, t, :], src).then_inc(params_in, 16)
            sp.wait_ge(dt_zero, 1)
            sp.dma_start(by_cols(raw[0])[:, :, 0:HEADS], w_dt).then_inc(slab_in[0], 16)
            load(sp, 1, 0, w_in_slabs[Z_SLABS + X_SLABS], by_cols)
            sp.wait_ge(x_T, DB)
            sp.wait_ge(par_T, 1)
            for j, src in enumerate((ssd_dt_bias, ssd_a_log, ssd_d)):
                sp.dma_start(heads_in[:, j, :], src[0:1, :].to_broadcast([P, HEADS])).then_inc(heads_loaded, 16)
            for s in range(1, BC_SLABS):
                load(sp, S_BC + s, 0, w_in_slabs[Z_SLABS + X_SLABS + s], by_cols)
            with sp.Fori(0, X_SLABS // 2) as i:
                for s in range(2):
                    load(sp, S_X + s, i, w_in_slabs[Z_SLABS + s + 2 * i], by_cols)
            with sp.Fori(0, Z_SLABS // 2) as i:
                for s in range(2):
                    load(sp, S_Z + s, i, w_in_slabs[s + 2 * i], by_cols)
            with sp.Fori(0, OUT_SLABS // 2) as i:
                for s in range(2):
                    load(sp, S_OUT + s, i, w_out_slabs[s + 2 * i], by_rows)
            for l in range(2):
                with sp.Fori(0, UP_SLABS // 2) as i:
                    for s in range(2):
                        load(sp, S_UP[l] + s, i, w_up_slabs[l][s * UP_SLABS // 2 + i], by_cols)
                with sp.Fori(0, DOWN_SLABS // 2) as i:
                    for s in range(2):
                        load(sp, S_DOWN[l] + s, i, w_down_slabs[l][s + 2 * i], by_rows)
                load(sp, S_DOWN[l] + DOWN_SLABS - 1, 0, w_down_slabs[l][DOWN_SLABS - 1], by_rows)
                if l == 0:
                    load(sp, S_POOL, 0, w_pool_slab,
                         lambda tile: tile[:].rearrange("p (g k n) -> p g k n", g=G, k=2))
            rows = out[0].rearrange("(c p) d -> p c d", p=P)
            for i, b in enumerate(ORDER):
                sp.wait_ge(out_copied, i + 1)
                sp.dma_start(rows[:, :, b * P:(b + 1) * P], out_rows[:, :, b * P:(b + 1) * P]).then_inc(out_stored, 16)
            sp.wait_ge(out_stored, 16 * DB)

        @block.gpsimd
        def _(pool):
            n = [0]

            def step(ins):
                n[0] += 1
                ins.then_inc(consts_step, 1)
                pool.wait_ge(consts_step, n[0])
            step(pool.memset(ident[:], 0.0))
            step(pool.memset(ones[:], 1.0))
            step(pool.memset(eps[:], EPS))
            step(pool.affine_select(out=ident[:], in_=ident[:], compare_op=ALU.not_equal, fill=1.0, base=0,
                                    pattern=[[-1, P]], channel_multiplier=1))
            step(pool.affine_select(out=upper[:], in_=ones[:], compare_op=ALU.is_ge, fill=0.0, base=0,
                                    pattern=[[1, P]], channel_multiplier=-1))
            pool.memset(par_rows[:, PAR_TILES - 1, :], 0.0).then_inc(consts, 1)
            pool.memset(raw[0][:], 0.0).then_inc(dt_zero, 1)
            step(pool.memset(edge[:], 1.0))
            for g, w in enumerate(POOL_WINDOWS):
                for t in range(w - 1):
                    step(pool.memset(edge[:, g, t:t + 1], w / (t + 1)))
            pool.wait_ge(x_T, DB)
            pool.wait_ge(par_T, 1)
            rows = decay[0:HPG, :, :].rearrange("r a (b n) -> r (a b) n", n=P)
            pool.memset(rows, 0.0).then_inc(sel_zero, 1)
            pool.wait_ge(sel_zero, 1)
            pool.affine_select(out=rows, in_=rows, compare_op=ALU.not_equal, fill=1.0, base=0,
                               pattern=[[-1, HPG], [0, P]], channel_multiplier=1).then_inc(sel_made, 1)
            pool.wait_ge(mm_done, 2 * S_POOL + MORE_POOL)
            pool.memset(win[:, :, 0:PAD], 0.0).then_inc(pads_zero, 1)

        @block.tensor
        def _(pe):
            prime(pe, "tensor")
            pe.wait_ge(consts, 1)
            pe.wait_ge(x_in, 16)
            for b in range(DB):
                for c in range(NCH):
                    mm = pe.transpose(bank[:, b, cs(c)], x_rows[:, c, b * P:(b + 1) * P], ident[:])
                mm.then_inc(x_T, 1)
            pe.wait_ge(params_in, 16 * len(par_pieces))
            pe.wait_ge(xres_ready, DB)
            for t in range(PAR_TILES):
                mm = pe.transpose(bank[:, t // 4, cs(t % 4)], par_rows[:, t, :], ident[:])
            mm.then_inc(par_T, 1)
            pe.wait_ge(par_ready, 1)
            norm_total(pe, 0)
            norm_spread(pe, 0)
            dt_product_pe(pe)
            for it in range(BC_SLABS // 2):
                xbc_pe(pe, S_BC + 2 * it, 0, it)
                if it == 0:
                    dt_transpose_pe(pe)
            dt_sums_pe(pe)
            with pe.Fori(0, X_SLABS // 2) as i:
                xbc_pe(pe, S_X, i, BC_SLABS // 2 + i)
            scan_pe(pe, 0, opening=True)
            with pe.Fori(0, G - 1) as g:
                scan_pe(pe, g)
            scan_pe(pe, G - 1, last=True)
            group_norm_pe(pe)
            for s in range(2):
                out_pe(pe, S_OUT + s, 0, 2 * s, first=s == 0)
            with pe.Fori(1, OUT_SLABS // 2 - 1) as i:
                for s in range(2):
                    out_pe(pe, S_OUT + s, i, 2 * s + 4 * i)
            for s in range(2):
                out_pe(pe, S_OUT + OUT_SLABS - 2 + s, 0, IB - 4 + 2 * s, last=s == 1)
            norm_total(pe, 1)
            norm_spread(pe, 1)
            for l in range(2):
                if l == 1:
                    pool_pe(pe)
                    norm_total(pe, 5)
                    norm_spread(pe, 5)
                up_first_pe(pe, l)
                with pe.Fori(1, UP_SLABS // 2) as i:
                    up_pe(pe, l, i)
                for s in range(2):
                    down_pe(pe, l, s, 0, first=s == 0)
                with pe.Fori(1, DOWN_SLABS // 2) as i:
                    for s in range(2):
                        down_pe(pe, l, s, i)
                down_pe(pe, l, DOWN_SLABS - 1, 0, last=True)
                norm_total(pe, 4 * l + 3)
                norm_spread(pe, 4 * l + 3)
            for i, b in enumerate(ORDER):
                pe.wait_ge(x_updated, 3 * DB + (i + 1 if i else 2))
                for c in range(NCH):
                    mm = pe.transpose(bank[:, b, cs(c)], xres[:, b, cs(c)], ident[:])
                mm.then_inc(out_T, 1)

        @block.scalar
        def _(act):
            prime(act, "scalar")
            for b in range(0, DB, 2):
                act.wait_ge(x_T, b + 1)
                act.activation(xres[:, b, :], bank[:, b, :], ACT.Copy).then_inc(xres_ready, 1)
            first_norm_act(act)
            dt_feat_act(act)
            for it in range(BC_SLABS // 2):
                xbc_act(act, S_BC + 2 * it, 0, it, IB + 4 * it, split=it == 0)
                if it == 0:
                    split_hi(act, S_BC + 3, 0)
                    dt_chain_act(act)
            with act.Fori(0, X_SLABS // 2) as i:
                xbc_act(act, S_X, i, BC_SLABS // 2 + i, 4 * i)
            dt_decays_act(act)
            scan_act(act, 0, opening=True)
            with act.Fori(0, G - 1) as g:
                scan_act(act, g)
            scan_act(act, G - 1, last=True)
            group_norm_act(act)
            group_scale_act(act, 0)
            for s in range(2):
                y_split_act(act, S_OUT + s, 0, 2 * s)
                if s == 0:
                    for g in range(1, G):
                        group_scale_act(act, g)
                split_hi(act, S_OUT + s + 1, 0)
            with act.Fori(1, OUT_SLABS // 2) as i:
                for s in range(2):
                    y_split_act(act, S_OUT + s, i, 2 * s + 4 * i)
                    split_hi(act, S_OUT + s + 1, i)
            boundary_act(act, 0, lambda b: (mm_done, 2 * (S_UP[0] - 1) + b + 1), more=(S_UP[0] + 1, MORE_UP[0]))
            for l in range(2):
                if l == 1:
                    boundary_act(act, 2, lambda b: (mixed, POOL_ORDER.index(b) + 1), lambda b: col("pool_scale", b),
                                 (S_UP[1] + 1, MORE_UP[1]))
                up_act(act, l, 0, split=False)
                with act.Fori(1, UP_SLABS // 2) as i:
                    up_act(act, l, i)
                with act.Fori(0, DOWN_SLABS // 2) as i:
                    for s in range(2):
                        split_hi(act, S_DOWN[l] + s + 1, i, MORE_UP[l])
                f_from = 2 * (S_DOWN[l] + DOWN_SLABS - 1) + MORE_UP[l]
                if l == 0:
                    split_hi(act, S_POOL, 0, MORE_UP[0])
                    boundary_act(act, 1, lambda b: (mm_done, f_from + b + 1), more=(S_UP[1], MORE_POOL))
                else:
                    boundary_act(act, 3, lambda b: (mm_done, f_from + b + 1), last=True)
            for i, b in enumerate(ORDER):
                act.wait_ge(out_T, i + 1)
                act.activation(out_rows[:, :, b * P:(b + 1) * P], chunked(bank[:, b, :]),
                               ACT.Copy).then_inc(out_copied, 1)

        @block.vector
        def _(dve):
            prime(dve, "vector")
            for b in range(1, DB, 2):
                dve.wait_ge(x_T, b + 1)
                dve.tensor_copy(xres[:, b, :], bank[:, b, :]).then_inc(xres_ready, 1)
            dve.wait_ge(par_T, 1)
            flat = bank[:, 0:2, :].rearrange("p b n -> p (b n)")
            dve.tensor_copy(par[:, :], flat[:, 0:PAR_TILES * P]).then_inc(par_ready, 1)
            dve.wait_ge(par_ready, 1)
            dve.tensor_tensor(pool_post[:, :], par[:, ROWS["pool_scale"]:ROWS["pool_scale"] + DB],
                              par[:, ROWS["mix_post"] + DB:ROWS["mix_post"] + 2 * DB], ALU.mult).then_inc(par_ready, 1)
            first_norm_dve(dve, norm_col("mix_pre", 0))
            for it in range(BC_SLABS // 2):
                xbc_dve(dve, S_BC + 2 * it, 0, it, IB + 4 * it, split=it == 0)
                if it == 0:
                    split_lo(dve, S_BC + 3, 0)
                    dt_chain_dve(dve)
            with dve.Fori(0, X_SLABS // 2) as i:
                xbc_dve(dve, S_X, i, BC_SLABS // 2 + i, 4 * i)
            dt_to_end_dve(dve)
            dve.wait_ge(dt_act, 7)
            scan_dve(dve, 0, opening=True)
            with dve.Fori(0, G - 1) as g:
                scan_dve(dve, g)
            scan_dve(dve, G - 1, last=True)
            group_norm_dve(dve)
            dve.wait_ge(group_scale_ready, 1)
            for s in range(2):
                y_split_dve(dve, S_OUT + s, 0, 2 * s, 0)
                split_lo(dve, S_OUT + s + 1, 0)
            dve.wait_ge(group_scale_ready, G)
            with dve.Fori(1, OUT_SLABS // 2) as i:
                for s in range(2):
                    y_split_dve(dve, S_OUT + s, i, 2 * s + 4 * i, i)
                    split_lo(dve, S_OUT + s + 1, i)
            boundary_dve(dve, 0, norm_col("mix_post", 0), norm_col("ffn_pre", 0), S_UP[0] + 1)
            for l in range(2):
                if l == 1:
                    pool_dve(dve)
                    dve.wait_ge(par_ready, 2)
                    boundary_dve(dve, 2, lambda b: pool_post[:, b:b + 1], norm_col("ffn_pre", 1), S_UP[1] + 1)
                up_dve(dve, l, 0, split=False)
                with dve.Fori(1, UP_SLABS // 2) as i:
                    up_dve(dve, l, i)
                with dve.Fori(0, DOWN_SLABS // 2) as i:
                    for s in range(2):
                        split_lo(dve, S_DOWN[l] + s + 1, i)
                if l == 0:
                    split_lo(dve, S_POOL, 0)
                    boundary_dve(dve, 1, norm_col("ffn_post", 0), norm_col("mix_pre", 1), S_UP[1])
                else:
                    boundary_dve(dve, 3, norm_col("ffn_post", 1))


_OUTPUT = (1, 512, 1024)
_INPUTS = ["x", "ssd_w_in", "ssd_conv_w", "ssd_conv_b", "ssd_dt_bias", "ssd_a_log", "ssd_d", "ssd_norm_w",
           "ssd_w_out", "pool_w", "pool_scale", "ffn_w_up", "ffn_conv_w", "ffn_conv_b", "ffn_w_down",
           "norm_mix_pre", "norm_mix_post", "norm_ffn_pre", "norm_ffn_post"]


def kernel(**inputs):
    import numpy as np
    import concourse.bacc as bacc
    from concourse.bass_utils import run_bass_kernel_spmd

    nc = bacc.Bacc("TRN2", target_bir_lowering=False, num_devices=1)
    arrays, args = {}, []
    for name in _INPUTS:
        a = np.ascontiguousarray(inputs[name])
        arrays[f"in_{name}"] = a
        args.append(nc.dram_tensor(f"in_{name}", a.shape, mybir.dt.from_np(a.dtype), kind="ExternalInput").ap())
    args.append(nc.dram_tensor("result", _OUTPUT, F32, kind="ExternalOutput").ap())
    hybrid_trunk(nc, *args)
    return run_bass_kernel_spmd(nc, [arrays], core_ids=[0]).results[0]["result"]
```
